# Optimizing a Trainium2 kernel written in Bass

```python
import jax, jax.numpy as jnp
from jax import lax
import numpy as np

D_MODEL = 1024
BATCH = 1
SEQ = 512
DEPTH = 2

N_MIXERS = 2
N_GLA = (DEPTH + 1) // 2
N_NSA = DEPTH // 2
NORM_EPS = 1e-6
ROPE_THETA = 10000.0
NEG = -1e30
BIG = 1e9

GLA_HEADS = 4
GLA_DK = D_MODEL // 2 // GLA_HEADS
GLA_DV = D_MODEL // GLA_HEADS
GLA_QK = GLA_HEADS * GLA_DK
GLA_V = GLA_HEADS * GLA_DV
GLA_GATE_RANK = 16
GLA_GATE_NORMALIZER = 16.0
GLA_CHUNK = 64
GLA_IN = 2 * GLA_QK + GLA_V + GLA_GATE_RANK + GLA_V

NSA_HEADS = 16
NSA_GROUPS = 4
NSA_HPG = NSA_HEADS // NSA_GROUPS
NSA_DH = D_MODEL // NSA_HEADS
NSA_Q = NSA_HEADS * NSA_DH
NSA_KV = NSA_GROUPS * NSA_DH
CMP_BLOCK = 32
CMP_STRIDE = 16
CMP_HIDDEN = 256
SEL_BLOCK = 64
SEL_TOP = 16
WINDOW = 512
Q_BLOCK = 64
NSA_IN = NSA_Q + 6 * NSA_KV + 3 * NSA_HEADS + NSA_Q


def rms_norm(x, g):
    xf = x.astype(jnp.float32)
    y = xf * lax.rsqrt(jnp.mean(xf * xf, axis=-1, keepdims=True) + NORM_EPS)
    return (y * g.astype(jnp.float32)).astype(x.dtype)

def rope(x, positions):
    dh = x.shape[-1]
    inv = ROPE_THETA ** (-jnp.arange(0, dh, 2, dtype=jnp.float32) / dh)
    ang = positions.astype(jnp.float32)[..., None] * inv
    cos = jnp.cos(ang)[:, :, None, :]
    sin = jnp.sin(ang)[:, :, None, :]
    x1, x2 = jnp.split(x, 2, axis=-1)
    return jnp.concatenate([x1 * cos - x2 * sin, x2 * cos + x1 * sin], axis=-1)

def gla_chunked(q, k, v, g):
    B, H, S, dk = q.shape
    dv = v.shape[-1]
    C = GLA_CHUNK
    N = S // C
    q = q.reshape(B, H, N, C, dk)
    k = k.reshape(B, H, N, C, dk)
    v = v.reshape(B, H, N, C, dv)
    b = jnp.cumsum(g.reshape(B, H, N, C, dk), axis=3)
    b_last = b[:, :, :, -1:]
    q_e = q * jnp.exp(b)
    k_e = k * jnp.exp(-b)
    k_d = k * jnp.exp(b_last - b)
    causal = jnp.tril(jnp.ones((C, C), dtype=bool))
    a = jnp.where(causal, jnp.einsum('bhnid,bhnjd->bhnij', q_e, k_e), 0.0)
    o_intra = jnp.einsum('bhnij,bhnjv->bhniv', a, v)

    def step(state, xs):
        qe, kd, vc, dec = xs
        o = jnp.einsum('bhcd,bhdv->bhcv', qe, state)
        state = dec[..., None] * state + jnp.einsum('bhcd,bhcv->bhdv', kd, vc)
        return state, o

    xs = (jnp.moveaxis(q_e, 2, 0), jnp.moveaxis(k_d, 2, 0), jnp.moveaxis(v, 2, 0),
          jnp.moveaxis(jnp.exp(b_last[:, :, :, 0]), 2, 0))
    _, o_inter = lax.scan(step, jnp.zeros((B, H, dk, dv), jnp.float32), xs)
    return (o_intra + jnp.moveaxis(o_inter, 0, 2)).reshape(B, H, S, dv)

def gla_mixer(h, w_in, w_gk_up, b_gk, head_norm, w_out):
    B, S, _ = h.shape
    p = (h @ w_in).astype(jnp.float32)
    q, k, v, glr, z = jnp.split(p, [GLA_QK, 2 * GLA_QK, 2 * GLA_QK + GLA_V,
                                    2 * GLA_QK + GLA_V + GLA_GATE_RANK], axis=-1)
    gk = jax.nn.log_sigmoid(glr @ w_gk_up.astype(jnp.float32) + b_gk.astype(jnp.float32)) / GLA_GATE_NORMALIZER

    def heads(t, d):
        return t.reshape(B, S, GLA_HEADS, d).transpose(0, 2, 1, 3)

    o = gla_chunked(heads(q, GLA_DK) * GLA_DK ** -0.5, heads(k, GLA_DK),
                    heads(v, GLA_DV), heads(gk, GLA_DK))
    o = rms_norm(o, head_norm)
    o = o.transpose(0, 2, 1, 3).reshape(B, S, GLA_V) * jax.nn.silu(z)
    return o @ w_out.astype(jnp.float32)

def compress(t, pe, w1, w2):
    B, S, G, DH = t.shape
    r = CMP_BLOCK // CMP_STRIDE
    nc = (S - CMP_BLOCK) // CMP_STRIDE + 1
    pieces = t.reshape(B, S // CMP_STRIDE, CMP_STRIDE, G, DH)
    blocks = jnp.concatenate([pieces[:, i:i + nc] for i in range(r)], axis=2)
    blocks = blocks + pe.astype(jnp.float32)[None, None, :, None, :]
    flat = blocks.transpose(0, 3, 1, 2, 4).reshape(B, G, nc, CMP_BLOCK * DH)
    return jax.nn.silu(flat @ w1.astype(jnp.float32)) @ w2.astype(jnp.float32)

def nsa_mixer(h, positions, w_in, b_gate, pe_k, pe_v, ck_w1, ck_w2, cv_w1, cv_w2, w_out):
    B, S, _ = h.shape
    G, HPG, DH = NSA_GROUPS, NSA_HPG, NSA_DH
    p = (h @ w_in).astype(jnp.float32)
    splits = [NSA_Q + i * NSA_KV for i in range(7)] + [NSA_Q + 6 * NSA_KV + 3 * NSA_HEADS]
    q, kc, vc, ks, vs, kw, vw, gl, z = jnp.split(p, splits, axis=-1)

    q = rope(q.reshape(B, S, NSA_HEADS, DH), positions) * DH ** -0.5
    kc = rope(kc.reshape(B, S, G, DH), positions)
    ks = rope(ks.reshape(B, S, G, DH), positions)
    kw = rope(kw.reshape(B, S, G, DH), positions)
    vc = vc.reshape(B, S, G, DH)
    vs = vs.reshape(B, S, G, DH)
    vw = vw.reshape(B, S, G, DH)

    kcmp = compress(kc, pe_k, ck_w1, ck_w2)
    vcmp = compress(vc, pe_v, cv_w1, cv_w2)
    nc = kcmp.shape[2]
    ns = S // SEL_BLOCK
    nq = S // Q_BLOCK
    n_top = min(SEL_TOP, ns)

    ksb = ks.reshape(B, ns, SEL_BLOCK, G, DH).transpose(0, 3, 1, 2, 4)
    vsb = vs.reshape(B, ns, SEL_BLOCK, G, DH).transpose(0, 3, 1, 2, 4)
    pad = ((0, 0), (0, 0), (WINDOW, 0), (0, 0))
    kwp = jnp.pad(kw.transpose(0, 2, 1, 3), pad)
    vwp = jnp.pad(vw.transpose(0, 2, 1, 3), pad)

    cmp_start = jnp.arange(nc) * CMP_STRIDE
    cmp_end = cmp_start + CMP_BLOCK - 1
    sel_start = jnp.arange(ns) * SEL_BLOCK
    overlap = ((cmp_start[:, None] < sel_start[None, :] + SEL_BLOCK) &
               (cmp_start[:, None] + CMP_BLOCK > sel_start[None, :])).astype(jnp.float32)
    jb = jnp.arange(ns)
    bidx = jnp.arange(B)[:, None, None, None]
    gidx = jnp.arange(G)[None, :, None, None]

    qblocks = q.reshape(B, nq, Q_BLOCK, G, HPG, DH).transpose(1, 0, 3, 4, 2, 5)

    def block(args):
        n, qb = args
        t = n * Q_BLOCK + jnp.arange(Q_BLOCK)
        s = jnp.einsum('bghtd,bgcd->bghtc', qb, kcmp)
        valid = cmp_end[None, :] <= t[:, None]
        pc = jax.nn.softmax(jnp.where(valid, s, NEG), axis=-1)
        pc = jnp.where(jnp.any(valid, axis=-1)[:, None], pc, 0.0)
        o_c = jnp.einsum('bghtc,bgcd->bghtd', pc, vcmp)
        imp = jnp.einsum('bghtc,cj->bgtj', pc, overlap)
        cur = (t // SEL_BLOCK)[:, None]
        forced = (jb[None] == 0) | (jb[None] == cur) | (jb[None] == cur - 1)
        causal_blk = sel_start[None, :] <= t[:, None]
        imp = jnp.where(forced, BIG, jnp.where(causal_blk, imp, NEG))
        _, idx = lax.top_k(imp, n_top)
        k_sel = ksb[bidx, gidx, idx]
        v_sel = vsb[bidx, gidx, idx]
        pos = idx[..., None] * SEL_BLOCK + jnp.arange(SEL_BLOCK)
        smask = (pos <= t[:, None, None])[:, :, None]
        s = jnp.where(smask, jnp.einsum('bghtd,bgtksd->bghtks', qb, k_sel), NEG)
        ps = jax.nn.softmax(s.reshape(B, G, HPG, Q_BLOCK, n_top * SEL_BLOCK), axis=-1).reshape(s.shape)
        o_s = jnp.einsum('bghtks,bgtksd->bghtd', ps, v_sel)
        kwin = lax.dynamic_slice_in_dim(kwp, n * Q_BLOCK, WINDOW + Q_BLOCK, axis=2)
        vwin = lax.dynamic_slice_in_dim(vwp, n * Q_BLOCK, WINDOW + Q_BLOCK, axis=2)
        wpos = n * Q_BLOCK - WINDOW + jnp.arange(WINDOW + Q_BLOCK)
        dlt = t[:, None] - wpos[None, :]
        wmask = (dlt >= 0) & (dlt < WINDOW) & (wpos[None, :] >= 0)
        s = jnp.where(wmask, jnp.einsum('bghtd,bgsd->bghts', qb, kwin), NEG)
        o_w = jnp.einsum('bghts,bgsd->bghtd', jax.nn.softmax(s, axis=-1), vwin)
        return jnp.stack([o_c, o_s, o_w], axis=0)

    out = lax.map(block, (jnp.arange(nq), qblocks))
    out = out.transpose(2, 0, 5, 3, 4, 1, 6).reshape(B, S, NSA_HEADS, 3, DH)
    gates = jax.nn.sigmoid(gl + b_gate.astype(jnp.float32)).reshape(B, S, NSA_HEADS, 3)
    o = jnp.einsum('bshc,bshcd->bshd', gates, out).reshape(B, S, NSA_Q) * jax.nn.silu(z)
    return o @ w_out.astype(jnp.float32)

def first_inputs(seed: int = 0) -> dict:
    key = jax.random.key(seed)
    ks = jax.random.split(key, 20)
    nrm = jax.random.normal
    f32 = jnp.float32
    return {
        "x": nrm(ks[0], (BATCH, SEQ, D_MODEL), f32),
        "positions": jnp.broadcast_to(jnp.arange(SEQ, dtype=jnp.int32), (BATCH, SEQ)),
        "pre_norm": 1.0 + 0.05 * nrm(ks[1], (DEPTH, D_MODEL), f32),
        "post_norm": 1.0 + 0.05 * nrm(ks[2], (DEPTH, D_MODEL), f32),
        "gla_w_in": nrm(ks[3], (N_GLA, D_MODEL, GLA_IN), f32) * D_MODEL ** -0.5,
        "gla_w_gk_up": nrm(ks[4], (N_GLA, GLA_GATE_RANK, GLA_QK), f32) * GLA_GATE_RANK ** -0.5,
        "gla_b_gk": 0.02 * nrm(ks[5], (N_GLA, GLA_QK), f32),
        "gla_head_norm": 1.0 + 0.05 * nrm(ks[6], (N_GLA, GLA_DV), f32),
        "gla_w_out": nrm(ks[7], (N_GLA, GLA_V, D_MODEL), f32) * GLA_V ** -0.5,
        "nsa_w_in": nrm(ks[8], (N_NSA, D_MODEL, NSA_IN), f32) * D_MODEL ** -0.5,
        "nsa_b_gate": 0.02 * nrm(ks[9], (N_NSA, 3 * NSA_HEADS), f32),
        "nsa_pe_k": 0.02 * nrm(ks[10], (N_NSA, CMP_BLOCK, NSA_DH), f32),
        "nsa_pe_v": 0.02 * nrm(ks[11], (N_NSA, CMP_BLOCK, NSA_DH), f32),
        "nsa_ck_w1": nrm(ks[12], (N_NSA, CMP_BLOCK * NSA_DH, CMP_HIDDEN), f32) * (CMP_BLOCK * NSA_DH) ** -0.5,
        "nsa_ck_w2": nrm(ks[13], (N_NSA, CMP_HIDDEN, NSA_DH), f32) * CMP_HIDDEN ** -0.5,
        "nsa_cv_w1": nrm(ks[14], (N_NSA, CMP_BLOCK * NSA_DH, CMP_HIDDEN), f32) * (CMP_BLOCK * NSA_DH) ** -0.5,
        "nsa_cv_w2": nrm(ks[15], (N_NSA, CMP_HIDDEN, NSA_DH), f32) * CMP_HIDDEN ** -0.5,
        "nsa_w_out": nrm(ks[16], (N_NSA, NSA_Q, D_MODEL), f32) * NSA_Q ** -0.5,
    }

def first_block(x, positions, pre_norm, post_norm, gla_w_in, gla_w_gk_up, gla_b_gk, gla_head_norm,
              gla_w_out, nsa_w_in, nsa_b_gate, nsa_pe_k, nsa_pe_v, nsa_ck_w1, nsa_ck_w2,
              nsa_cv_w1, nsa_cv_w2, nsa_w_out):
    for i in range(DEPTH):
        h = rms_norm(x, pre_norm[i])
        j = i // N_MIXERS
        if i % N_MIXERS == 0:
            y = gla_mixer(h, gla_w_in[j], gla_w_gk_up[j], gla_b_gk[j], gla_head_norm[j], gla_w_out[j])
        else:
            y = nsa_mixer(h, positions, nsa_w_in[j], nsa_b_gate[j], nsa_pe_k[j], nsa_pe_v[j],
                          nsa_ck_w1[j], nsa_ck_w2[j], nsa_cv_w1[j], nsa_cv_w2[j], nsa_w_out[j])
        x = x + rms_norm(y.astype(x.dtype), post_norm[i])
    return x


DEPTH_2 = 1

N_HEADS = 16
HEAD_DIM = D_MODEL // N_HEADS
D_ATTN = N_HEADS * HEAD_DIM
BLOCK_Q = 128
SB_SCALE = HEAD_DIM ** -0.5
POOL_WINDOWS = (2, 4, 8, 16)
N_POOL_GROUPS = len(POOL_WINDOWS)
D_POOL = D_MODEL
POOL_GROUP_DIM = D_POOL // N_POOL_GROUPS
SPLITS = (D_ATTN, D_ATTN, D_ATTN, D_ATTN, D_POOL, D_POOL, D_MODEL, D_MODEL)
IN_COLS = sum(SPLITS)
EPS = 1e-6


def rms_norm_2(x, gain):
    xf = x.astype(jnp.float32)
    y = xf * lax.rsqrt(jnp.mean(xf * xf, axis=-1, keepdims=True) + EPS)
    return (y * gain.astype(jnp.float32)).astype(x.dtype)

def stick_breaking_attention(q, k, v):
    S = q.shape[2]
    outs = []
    for i in range(S // BLOCK_Q):
        q0, q1 = i * BLOCK_Q, (i + 1) * BLOCK_Q
        qb = q[:, :, q0:q1]
        kb = k[:, :, :q1]
        vb = v[:, :, :q1]
        z = jnp.einsum('bhqd,bhkd->bhqk', qb, kb).astype(jnp.float32) * SB_SCALE
        q_pos = jnp.arange(q0, q1)[:, None]
        k_pos = jnp.arange(q1)[None, :]
        mask = k_pos < q_pos
        log_1m_beta = jnp.where(mask, -jax.nn.softplus(z), 0.0)
        suffix = lax.cumsum(log_1m_beta, axis=3, reverse=True) - log_1m_beta
        w = jnp.where(mask, jnp.exp(jax.nn.log_sigmoid(z) + suffix), 0.0)
        outs.append(jnp.einsum('bhqk,bhkd->bhqd', w.astype(vb.dtype), vb))
    return jnp.concatenate(outs, axis=2)

def multiscale_causal_pool(u, pool_w, pool_scale):
    B, S, _ = u.shape
    uf = u.astype(jnp.float32)
    pos_count = jnp.arange(S) + 1
    diffs = []
    for g, win in enumerate(POOL_WINDOWS):
        ug = uf[:, :, g * POOL_GROUP_DIM:(g + 1) * POOL_GROUP_DIM]
        cs = jnp.cumsum(ug, axis=1)
        cs_shift = jnp.pad(cs, ((0, 0), (win, 0), (0, 0)))[:, :S]
        count = jnp.minimum(pos_count, win).astype(jnp.float32)[None, :, None]
        diffs.append((cs - cs_shift) / count - ug)
    d = jnp.stack(diffs, axis=2).astype(u.dtype)
    mixed = jnp.einsum('bsgc,gcd->bsgd', d, pool_w).reshape(B, S, D_POOL)
    return mixed * pool_scale

def hybrid_layer(x, c, norm_gain, w_ada, b_ada, w_in, pool_w, pool_scale,
                 w_branch_a, w_branch_b, w_out):
    B, S, D = x.shape
    mod = jax.nn.silu(c) @ w_ada + b_ada
    shift, scale, gate = jnp.split(mod, 3, axis=-1)
    h = rms_norm_2(x, norm_gain) * (1.0 + scale[:, None, :]) + shift[:, None, :]

    proj = h @ w_in
    offs = np.cumsum(SPLITS)[:-1].tolist()
    q, k, v, z_a, u, z_b, m_a, m_b = jnp.split(proj, offs, axis=-1)

    to_heads = lambda t: t.reshape(B, S, N_HEADS, HEAD_DIM).transpose(0, 2, 1, 3)
    attn = stick_breaking_attention(to_heads(q), to_heads(k), to_heads(v))
    attn = attn.transpose(0, 2, 1, 3).reshape(B, S, D_ATTN)
    p_a = (attn * jax.nn.silu(z_a)) @ w_branch_a

    pooled = multiscale_causal_pool(u, pool_w, pool_scale)
    p_b = (pooled * jax.nn.silu(z_b)) @ w_branch_b

    merged = jax.nn.sigmoid(m_a) * p_a + jax.nn.sigmoid(m_b) * p_b
    out = merged @ w_out
    return x + gate[:, None, :] * out

def second_inputs(seed: int = 0) -> dict:
    key = jax.random.key(seed)
    ks = jax.random.split(key, 13)
    f32 = jnp.float32
    nrm = lambda k, shape, s: jax.random.normal(k, shape, f32) * s
    return {
        "x": nrm(ks[0], (BATCH, SEQ, D_MODEL), 1.0),
        "c": nrm(ks[1], (BATCH, D_MODEL), 1.0),
        "norm_gain": 1.0 + nrm(ks[2], (DEPTH_2, D_MODEL), 0.05),
        "w_ada": nrm(ks[3], (DEPTH_2, D_MODEL, 3 * D_MODEL), 0.5 * D_MODEL ** -0.5),
        "b_ada": nrm(ks[4], (DEPTH_2, 3 * D_MODEL), 0.01),
        "w_in": nrm(ks[5], (DEPTH_2, D_MODEL, IN_COLS), D_MODEL ** -0.5),
        "pool_w": nrm(ks[6], (DEPTH_2, N_POOL_GROUPS, POOL_GROUP_DIM, POOL_GROUP_DIM), POOL_GROUP_DIM ** -0.5),
        "pool_scale": 1.0 + nrm(ks[7], (DEPTH_2, D_POOL), 0.1),
        "w_branch_a": nrm(ks[8], (DEPTH_2, D_ATTN, D_MODEL), D_ATTN ** -0.5),
        "w_branch_b": nrm(ks[9], (DEPTH_2, D_POOL, D_MODEL), D_POOL ** -0.5),
        "w_out": nrm(ks[10], (DEPTH_2, D_MODEL, D_MODEL), D_MODEL ** -0.5),
        "final_gain": 1.0 + nrm(ks[11], (D_MODEL,), 0.05),
    }

def second_block(x, c, norm_gain, w_ada, b_ada, w_in, pool_w, pool_scale,
              w_branch_a, w_branch_b, w_out, final_gain):
    for l in range(DEPTH_2):
        x = hybrid_layer(x, c, norm_gain[l], w_ada[l], b_ada[l], w_in[l], pool_w[l],
                         pool_scale[l], w_branch_a[l], w_branch_b[l], w_out[l])
    return rms_norm_2(x, final_gain)


def setup_inputs(seed=0):
    out = dict(first_inputs(seed))
    for name, value in second_inputs(seed + 1).items():
        if name != "x":
            out[name + "_2"] = value
    return out


def reference(
    x, positions, pre_norm, post_norm, gla_w_in, gla_w_gk_up, gla_b_gk, gla_head_norm,
    gla_w_out, nsa_w_in, nsa_b_gate, nsa_pe_k, nsa_pe_v, nsa_ck_w1, nsa_ck_w2, nsa_cv_w1,
    nsa_cv_w2, nsa_w_out, c_2, norm_gain_2, w_ada_2, b_ada_2, w_in_2, pool_w_2, pool_scale_2,
    w_branch_a_2, w_branch_b_2, w_out_2, final_gain_2,
):
    x = first_block(
        x, positions, pre_norm, post_norm, gla_w_in, gla_w_gk_up, gla_b_gk, gla_head_norm,
        gla_w_out, nsa_w_in, nsa_b_gate, nsa_pe_k, nsa_pe_v, nsa_ck_w1, nsa_ck_w2, nsa_cv_w1,
        nsa_cv_w2, nsa_w_out,
    )
    return second_block(
        x, c_2, norm_gain_2, w_ada_2, b_ada_2, w_in_2, pool_w_2, pool_scale_2, w_branch_a_2,
        w_branch_b_2, w_out_2, final_gain_2,
    )


_drawn_inputs = setup_inputs


def setup_inputs(seed=0):
    import zlib

    import numpy as np

    out = dict(_drawn_inputs(seed))
    spreads = {}
    factors = {'gla_b_gk': 7.328,
     'nsa_b_gate': 8.0,
     'nsa_pe_k': 8.0,
     'nsa_pe_v': 2.81,
     'norm_gain_2': 8.0,
     'b_ada_2': 8.0,
     'pool_scale_2': 8.0}
    for name, (base, spread) in spreads.items():
        noise = np.random.default_rng([zlib.crc32(name.encode()), seed]).standard_normal(out[name].shape)
        drawn = base * np.exp(spread * noise) if base else spread * noise
        out[name] = __import__('jax').numpy.asarray(drawn.astype(out[name].dtype))
    for name, factor in factors.items():
        out[name] = (out[name] * factor).astype(out[name].dtype)
    return out
```

```python
from contextlib import ExitStack

import numpy as np

import concourse.bass as bass
from concourse import mybir
from concourse.alu_op_type import AluOpType as ALU

ACT = mybir.ActivationFunctionType
F32 = mybir.dt.float32
F32R = mybir.dt.float32r
I32 = mybir.dt.int32
U32 = mybir.dt.uint32
AX_X = mybir.AxisListType.X

P = 128
D = 1024
S = 512
KT = D // P
TT = S // P
CW = 256
NEG = -1e30
EPS = 1e-6

GH, GDK, GDV, GC = 4, 128, 256, 64
GN = S // GC
G_Q, G_K, G_V, G_R, G_Z = 0, 512, 1024, 2048, 2064
GNORM = 16.0
CAP = 44.0

NG, NHG, NDH = 4, 4, 64
NC, NCP = 31, 32
CB, CS = 32, 16
KV_PAD = 528
N_Q, N_KC, N_VC, N_KS, N_VS, N_KW, N_VW, N_GL, N_Z = 0, 1024, 1280, 1536, 1792, 2048, 2304, 2560, 2608
ROUND = 1.5 * 2.0 ** 23
TWO_PI = (6.28125, 0.0019350051879882812, 3.0199159819567e-07)
PI_DOWN = 3.1415925

HH = 16
H_Q, H_K, H_V, H_ZA, H_U, H_ZB, H_MA, H_MB = range(0, 8 * D, D)
WINDOWS = (2, 4, 8, 16)

VECS = [("pre0", 8), ("pre1", 8), ("post0", 8), ("post1", 8), ("gain2", 8), ("final", 8), ("b_ada", 24),
        ("pool_scale", 8), ("c", 8), ("b_gk", 4), ("head_norm", 2)]
VAT = {}
_n = 0
for _name, _k in VECS:
    VAT[_name] = _n
    _n += _k
NVEC = _n


N_SMALL2 = 7
NPAIR = TT * 8
MOD_PAIR = 24


def build_program(nc, A, out):
    es = ExitStack()
    with es:
        mem = [nc.sbuf_base + 64 - nc.sbuf_base % 64]

        def sb(name, shape, dt=F32):
            n = 1
            for x in shape[1:]:
                n *= x
            n *= 4
            t = nc.alloc_sbuf_tensor_at(name, list(shape), dt, offset=mem[0])
            mem[0] += (n + 31) // 32 * 32
            assert mem[0] <= nc.sbuf_usable_end, (name, mem[0], nc.sbuf_usable_end)
            return t

        def sem(name):
            return es.enter_context(nc.semaphore(name))

        banks = es.enter_context(nc.psum_tensor("banks", [P, 8, S], F32))
        bank = [banks[:, i, :] for i in range(8)]

        xT = sb("xT", [P, KT, S])
        act_hi = sb("act_hi", [P, KT, S], F32R)
        act_lo = sb("act_lo", [P, KT, S], F32R)
        raw = sb("raw", [P, 2, KT, CW])
        w_hi = sb("w_hi", [P, 2, KT, CW], F32R)
        w_lo = sb("w_lo", [P, 2, KT, CW], F32R)
        ident = sb("ident", [P, P])
        ones = sb("ones", [P, P])
        vec = sb("vec", [P, NVEC])
        eps_col = sb("eps_col", [P, 1])
        mod = sb("mod", [P, 3 * KT])
        silu_c = sb("silu_c", [P, KT])
        tmp = sb("tmp", [P, 2, S])
        rstd = sb("rstd", [P, S])
        arena = mem[0]

        qk = sb("qk", [P, 2 * GH, S])
        gate_b = sb("gate_b", [P, GH, S])
        kd_t = sb("kd_t", [P, GH, S])
        v_tok = sb("v_tok", [P, TT, D])
        silu_z = sb("silu_z", [P, KT, S])
        att = sb("att", [P, GH, S])
        kd_tok = sb("kd_tok", [P, GH, TT, P])
        states = sb("states", [P, 2, GN, GDV])
        decay = sb("decay", [P, GH, GN])
        neg_bgk = sb("neg_bgk", [P, GH])
        causal = sb("causal", [P, P], U32)
        chunk_keep = sb("chunk_keep", [P, S])
        glr_t = sb("glr_t", [16, S])
        w_up = sb("w_up", [16, S])
        head_sel = sb("head_sel", [P, 2 * GH - 1])


        def over(name, shape, base, dt=F32, at=None):
            return nc.alloc_sbuf_tensor_at(name, shape, dt, offset=base.manual_sbuf_range[0] if at is None else at)

        x_tok = over("x_tok", [P, TT, D], v_tok)
        vec_rows = over("vec_rows", [P, P], silu_z)
        y_t = over("y_t", [P, KT, S], qk)
        y_sq = over("y_sq", [P, KT, S], silu_z)
        o_t = over("o_t", [P, KT, S], gate_b)
        exps = over("exps", [P, 2, 3, S], states)
        head_std = over("head_std", [P, S], kd_tok)

        mem[0] = arena
        qT = sb("qT", [P, 8, S])
        silu_z2 = sb("silu_z2", [P, TT, D])
        kv_full = sb("kv_full", [P, NG, KV_PAD])
        rope_a = sb("rope_a", [P, 2, S])
        rope_b = sb("rope_b", [P, 2, S])
        kv_hi = sb("kv_hi", [P, NG + 1, KV_PAD], F32R)
        kv_lo = sb("kv_lo", [P, NG + 1, KV_PAD], F32R)
        ksT = sb("ksT", [P, 2, S])
        kwT = sb("kwT", [P, 2, S])
        v_tok2 = sb("v_tok2", [P, TT, 2, CW])
        cosT, sinT = sb("cosT", [P, S]), sb("sinT", [P, S])
        perm = sb("perm", [P, P])
        identb, maskb = sb("identb", [P, P], mybir.dt.bfloat16), sb("maskb", [P, P], mybir.dt.bfloat16)
        gates = sb("gates", [P, TT, 48])
        gate_bias = sb("gate_bias", [P, 48])
        rope_c = sb("rope_c", [P, 2])
        pe_t = sb("pe_t", [P, 2, CB // 2])
        hid_bias = sb("hid_bias", [P, 2])
        hid = sb("hid", [P, 2, NG * NCP])
        w2k, w2v = sb("w2k", [P, 2, NDH]), sb("w2v", [P, 2, NDH])
        kcmpT = sb("kcmpT", [P, NG * NCP])
        vcmp = sb("vcmp", [P, NG, CW])
        cmask = sb("cmask", [P, TT, NCP])
        cvalid = sb("cvalid", [P, TT, NCP])
        pcT = sb("pcT", [P, NG, P])
        cstat = sb("cstat", [P, 3, 16])
        wstat = sb("wstat", [P, 4, 2, 4])
        o_tok = over("o_tok", [P, TT, D], kv_full)
        prob = over("prob", [P, 3, 2, S], kv_hi)
        probT = over("probT", [P, 2, 2, S], None, at=kv_hi.manual_sbuf_range[0] + 4 * 3 * 2 * S)
        y_t2 = over("y_t2", [P, KT, S], qT)
        y_sq2 = over("y_sq2", [P, KT, S], silu_z2)
        csc = tmp[:]
        hid4 = tmp[:]
        ada_sum = over("ada_sum", [P, 12, CW], w_lo)
        wide_zero = pcT[:, 0, :]
        pe_rows = pcT[0:CB, 1, :]

        mem[0] = arena
        br_hi, br_lo = sb("br_hi", [P, KT, S], F32R), sb("br_lo", [P, KT, S], F32R)
        qh, kh = sb("qh", [P, 2, 2, S]), sb("kh", [P, 2, 2, S])
        vh, zh = sb("vh", [P, 2, TT, CW]), sb("zh", [P, 2, 2, S])
        mix_a = sb("mix_a", [P, KT, S])
        ln_z = sb("ln_z", [P, 10, P])
        sp_z = sb("sp_z", [P, 10, P])
        w_z = sb("w_z", [P, 10, P])
        gated = sb("gated", [P, 2, S])
        tri = sb("tri", [P, P])
        minus = sb("minus", [P, P])
        identb3, maskb3 = sb("identb3", [P, P], mybir.dt.bfloat16), sb("maskb3", [P, P], mybir.dt.bfloat16)
        pool_fix = sb("pool_fix", [P, 4, 16])
        gain_mod = sb("gain_mod", [P, KT])
        pool_u = over("pool_u", [P, KT, S], qh)
        silu_zb = over("silu_zb", [P, KT, S], vh)
        mix_b = over("mix_b", [P, KT, S], ln_z)
        sums = [over("sums0", [P, 2, S], ln_z), over("sums1", [P, 2, S], sp_z)]
        out_tok = over("out_tok", [P, TT, D], qh)

        consts_ready = sem("consts_ready")
        x_landed, vec_landed, up_landed = sem("x_landed"), sem("vec_landed"), sem("up_landed")
        raw_landed = [sem(f"raw_landed{i}") for i in range(2)]
        hi_done, lo_done = sem("hi_done"), sem("lo_done")
        bank_full = [sem(f"bank_full{i}") for i in range(4)]
        bank_free = [sem(f"bank_free{i}") for i in range(4)]
        xt_full, xt_copied, vec_full, vec_ready = sem("xt_full"), sem("xt_copied"), sem("vec_full"), sem("vec_ready")
        sq_ready, sq_used, rstd_ready = sem("sq_ready"), sem("sq_used"), sem("rstd_ready")
        scaled, act_hi_done, h_ready = sem("scaled"), sem("act_hi_done"), sem("h_ready")
        x_updated = sem("x_updated")
        dve_chain = sem("dve_chain")
        act_chain = sem("act_chain")
        pool_chain = sem("pool_chain")
        glr_copied, up_full, nu_ready, ln_ready = sem("glr_copied"), sem("up_full"), sem("nu_ready"), sem("ln_ready")
        gsum_ready, grow_ready, exps_ready, exps_used = sem("gsum_ready"), sem("grow_ready"), sem("exps_ready"), sem("exps_used")
        kd_ready, kdt_full, kdtok_ready = sem("kd_ready"), sem("kdt_full"), sem("kdtok_ready")
        att_full, att_ready = sem("att_full"), sem("att_ready")
        upd_full, upd_read, state_ready = sem("upd_full"), sem("upd_read"), sem("state_ready")
        o_full, o_squared, o_read = sem("o_full"), sem("o_squared"), sem("o_read")
        osq_used, orstd_ready, obc_full = sem("osq_used"), sem("orstd_ready"), sem("obc_full")
        out_full, out_left, out_right, stored = sem("out_full"), sem("out_left"), sem("out_right"), sem("stored")

        small2_landed, consts2_ready = sem("small2_landed"), sem("consts2_ready")
        pe_full, pe_ready = sem("pe_full"), sem("pe_ready")
        angle_ready, table_ready = sem("angle_ready"), sem("table_ready")
        turn_ready, turn_full, turned = sem("turn_ready"), sem("turn_full"), sem("turned")
        kv_ready, kv_hi_done, kv_split = sem("kv_ready"), sem("kv_hi_done"), sem("kv_split")
        hid_bias_ready, hid_ready = sem("hid_bias_ready"), sem("hid_ready")
        cmp_full, cmp_ready = sem("cmp_full"), sem("cmp_ready")
        gate_sum, gate_ready = sem("gate_sum"), sem("gate_ready")
        c_scores, c_shifted, c_exp, c_prob = sem("c_scores"), sem("c_shifted"), sem("c_exp"), sem("c_prob")
        c_tfull, c_tcopied, c_out, c_taken = sem("c_tfull"), sem("c_tcopied"), sem("c_out"), sem("c_taken")
        s_full, s_max, s_exp = sem("s_full"), sem("s_max"), sem("s_exp")
        t_full, t_sel, t_win = sem("t_full"), sem("t_sel"), sem("t_win")
        pv_full, pv_read, o_gated = sem("pv_full"), sem("pv_read"), sem("o_gated")
        ot_full, ot_high, ot_low = sem("ot_full"), sem("ot_high"), sem("ot_low")

        silu_c_ready, ada_summed, mod_full, mod_ready = sem("silu_c_ready"), sem("ada_summed"), sem("mod_full"), sem("mod_ready")
        consts3_ready, small3_landed = sem("consts3_ready"), sem("small3_landed")
        z_full, zc_ready, e_ready, l_ready, sp_ready = sem("z_full"), sem("zc_ready"), sem("e_ready"), sem("l_ready"), sem("sp_ready")
        tri_full, w_ready, hv_full, head_gated = sem("tri_full"), sem("w_ready"), sem("hv_full"), sem("head_gated")
        pair_high, pair_low = sem("pair_high"), sem("pair_low")
        d_ready, d_high, d_low, mix_full, mix_taken = sem("d_ready"), sem("d_high"), sem("d_low"), sem("mix_full"), sem("mix_taken")
        x_final, fin_ready = sem("x_final"), sem("fin_ready")

        def cols(m, at, n=CW):
            return m[:, bass.ds(at, n)].rearrange("(k p) n -> p k n", p=P)

        C_GLR, C_Q, C_K, C_V, C_Z, C_GOUT = 0, 1, 3, 5, 9, 13
        C_KC, C_KS, C_VC, C_KW, C_CK, C_VS, C_VW, C_CV, C_GL, C_NQ, C_NZ, C_ADA, C_NOUT = (
            17, 18, 19, 20, 21, 23, 24, 25, 27, 28, 32, 36, 48)
        C_H, C_MA, C_U, C_BA, C_ZB, C_MB, C_MIX, C_BB, C_OUT = 52, 68, 72, 76, 80, 84, 88, 89, 93
        C_END = 97
        w3 = A["w_in_2"]
        w2, wo2, ck, cv = A["nsa_w_in"], A["nsa_w_out"], A["nsa_ck_w1"], A["nsa_cv_w1"]
        w1, wo1 = A["gla_w_in"], A["gla_w_out"]
        groups = [(C_GLR, 1, w1, G_R), (C_Q, 2, w1, G_Q), (C_K, 2, w1, G_K), (C_V, 4, w1, G_V),
                  (C_Z, 4, w1, G_Z), (C_GOUT, 4, wo1, 0)]
        groups2 = [(C_KC, 1, w2, N_KC), (C_KS, 1, w2, N_KS), "small", (C_VC, 1, w2, N_VC), (C_KW, 1, w2, N_KW),
                   (C_CK, 2, ck, None), (C_VS, 1, w2, N_VS), (C_VW, 1, w2, N_VW), (C_CV, 2, cv, None),
                   (C_GL, 1, w2, N_GL), (C_NQ, 4, w2, "q"), (C_NZ, 4, w2, N_Z), (C_ADA, 12, A["w_ada_2"], 0), (C_NOUT, 4, wo2, 0)]
        groups3 = [(C_MA, 4, w3, H_MA), "small", (C_U, 4, w3, H_U), (C_BA, 4, A["w_branch_a_2"], 0),
                   (C_ZB, 4, w3, H_ZB), (C_MB, 4, w3, H_MB), (C_MIX, 1, A["pool_w_2"], 0),
                   (C_BB, 4, A["w_branch_b_2"], 0), (C_OUT, 4, A["w_out_2"], 0)]

        def vcol(name, j):
            return vec[:, VAT[name] + j:VAT[name] + j + 1]

        def blocks(x, st):
            at = (0, 4, 7, 9)[st]
            return x[:, at:at + TT - st].rearrange("p b q -> p (b q)")

        def banks_free(eng, c):
            for b in range(4):
                eng.wait_ge(bank_free[b], (c + 1 - b // 2) // 2)

        def update_at(n):
            return bank[4 + 2 * (n % 2) + n // 4][:, n // 2 % 2 * GDV:(n // 2 % 2 + 1) * GDV]

        block = es.enter_context(nc.Block())

        @block.sync
        def _(sp):
            sp.dma_start(x_tok[:], A["x"].rearrange("(t p) d -> p t d", p=P)).then_inc(x_landed, 16)
            for name, n in VECS:
                sp.dma_start(vec_rows[VAT[name]:VAT[name] + n, :],
                             A[name].rearrange("(k p) -> k p", p=P)).then_inc(vec_landed, 16)
            sp.dma_start(w_up[:], A["gla_w_gk_up"]).then_inc(up_landed, 16)

            def load(c, u, m, at):
                if not (isinstance(c, int) and c < 2):
                    sp.wait_ge(lo_done, c - 1)
                sp.dma_start(raw[:, u], cols(m, at)).then_inc(raw_landed[u], 16)

            for c0, n, m, at in groups:
                if n < 4 or c0 < 2:
                    for j in range(n):
                        load(c0 + j, (c0 + j) % 2, m, at + j * CW)
                else:
                    with sp.Fori(0, n // 2) as i:
                        for u in range(2):
                            load(2 * i + (c0 + u), (c0 + u) % 2, m, 2 * CW * i + (at + u * CW))
            for group in groups2:
                if group == "small":
                    sp.wait_ge(x_updated, KT)
                    pos = A["positions"].rearrange("(o s) -> o s", o=1).broadcast_to([P, S])
                    small = [(rope_a[:, 0].bitcast(I32), pos), (rope_c[:], A["rope_const"]),
                             (gate_bias[:], A["nsa_b_gate"].rearrange("(o s) -> o s", o=1).broadcast_to([P, 48]))]
                    small += [(w[:], A[n].rearrange("(k p) d -> p k d", p=P)) for w, n in ((w2k, "nsa_ck_w2"), (w2v, "nsa_cv_w2"))]
                    small += [(pe_rows[CB // 2 * i:CB // 2 * (i + 1), :], A[n].rearrange("(m h) d -> m (h d)", h=2))
                              for i, n in enumerate(("nsa_pe_k", "nsa_pe_v"))]
                    assert len(small) == N_SMALL2
                    for dst, src in small:
                        sp.dma_start(dst, src).then_inc(small2_landed, 16)
                    continue
                c0, n, m, at = group
                if at == "q":
                    for j in range(4):
                        u = (c0 + j) % 2
                        sp.wait_ge(lo_done, c0 + j - 1)
                        for h in range(2):
                            for g in range(2):
                                sp.dma_start(raw[:, u, :, h * P + g * NDH:h * P + (g + 1) * NDH],
                                             cols(m, j // 2 * 512 + g * CW + (j % 2 * 2 + h) * NDH, NDH))\
                                    .then_inc(raw_landed[u], 16)
                elif at is None:
                    for j in range(2):
                        sp.wait_ge(lo_done, c0 + j - 1)
                        sp.dma_start(raw[:, (c0 + j) % 2], m[j * D:(j + 1) * D, :].rearrange("(k p) n -> p k n", p=P))\
                            .then_inc(raw_landed[(c0 + j) % 2], 16)
                elif n < 4:
                    load(c0, c0 % 2, m, at)
                else:
                    with sp.Fori(0, n // 2) as i:
                        for u in range(2):
                            load(2 * i + (c0 + u), (c0 + u) % 2, m, 2 * CW * i + (at + u * CW))
            for kind, at in enumerate((H_Q, H_K, H_V, H_ZA)):
                load(C_H + kind, (C_H + kind) % 2, w3, at)
            with sp.Fori(0, 3) as i:
                for kind, at in enumerate((H_Q, H_K, H_V, H_ZA)):
                    load(4 * i + (C_H + 4 + kind), (C_H + kind) % 2, w3, CW * i + (at + CW))
            for group in groups3:
                if group == "small":
                    sp.wait_ge(x_updated, 2 * KT)
                    fix = A["pool_const"].rearrange("(o g) t -> o g t", o=1).broadcast_to([P, 4, 16])
                    sp.dma_start(pool_fix[:], fix).then_inc(small3_landed, 16)
                    continue
                c0, n, m, at = group
                if n < 4:
                    load(c0, c0 % 2, m, at)
                else:
                    with sp.Fori(0, n // 2) as i:
                        for u in range(2):
                            load(2 * i + (c0 + u), (c0 + u) % 2, m, 2 * CW * i + (at + u * CW))
            for t in range(TT):
                sp.wait_ge(out_left, t + 1)
                sp.wait_ge(out_right, t + 1)
                sp.dma_start(out[t * P:(t + 1) * P, :], out_tok[:, t, :]).then_inc(stored, 16)
            sp.wait_ge(stored, 16 * TT)

        @block.gpsimd
        def _(pool):
            chained = [0]

            def link(ins):
                chained[0] += 1
                ins.then_inc(pool_chain, 1)
                pool.wait_ge(pool_chain, chained[0])

            pool.memset(ones[:], 1.0)
            pool.memset(eps_col[:], EPS)
            pool.memset(head_sel[:], 0.0)
            pool.memset(att[:], 0.0)
            pool.memset(chunk_keep[:], 1.0)
            link(pool.memset(ident[:], 0.0))
            pool.memset(head_sel[:, GH - 1:GH], 1.0)
            pool.memset(chunk_keep[:].rearrange("p (n c) -> p n c", c=GC)[:, :, 0:1], 0.0)
            link(pool.affine_select(out=ident[:], in_=ident[:], compare_op=ALU.not_equal, fill=1.0, base=0,
                                    pattern=[[-1, P]], channel_multiplier=1))
            link(pool.affine_select(out=tmp[:, 0, 0:P], in_=ones[:], compare_op=ALU.is_ge, fill=0.0, base=0,
                                    pattern=[[1, P]], channel_multiplier=-1))
            link(pool.memset(tmp[0:GC, 0, GC:P], 0.0))
            link(pool.tensor_copy(causal[:], tmp[:, 0, 0:P]))
            pool.memset(rstd[:, 0:1], 0.0).then_inc(consts_ready, 1)

            def split_low(c, u):
                pool.wait_ge(hi_done, c + 1)
                pool.tensor_tensor(w_lo[:, u], raw[:, u], w_hi[:, u].bitcast(F32), ALU.subtract).then_inc(lo_done, 1)

            def split_range(c0, c1):
                pairs = (c1 - c0) // 2
                if pairs > 1:
                    with pool.Fori(0, pairs) as i:
                        for u in range(2):
                            split_low(2 * i + (c0 + u), (c0 + u) % 2)
                    c0 += 2 * pairs
                for c in range(c0, c1):
                    split_low(c, c % 2)

            split_range(0, C_KC + 1)
            pool.wait_ge(x_updated, KT)
            pool.memset(kv_full[:], 0.0)
            pool.memset(vcmp[:], 0.0)
            link(pool.memset(cvalid[:], 1.0))
            link(pool.affine_select(out=cvalid[:], in_=cvalid[:], compare_op=ALU.is_ge, fill=0.0, base=1 - CB,
                                    pattern=[[P, TT], [-CS, NCP]], channel_multiplier=1))
            pool.tensor_scalar(cmask[:], cvalid[:], -1.0, -NEG, ALU.add, ALU.mult)
            for t in range(2):
                two = lambda a: a.rearrange("p (a two w) -> p a two w", two=2, w=32)
                pool.tensor_copy(two(perm[:])[:, :, t], two(ident[:])[:, :, 1 - t])
            pool.tensor_copy(identb[:], ident[:])
            link(pool.memset(wide_zero, 0.0))
            link(pool.affine_select(out=wide_zero, in_=wide_zero, compare_op=ALU.is_ge, fill=NEG, base=0,
                                    pattern=[[-1, P]], channel_multiplier=1))
            pool.tensor_copy(maskb[:], wide_zero)
            pool.memset(kv_hi[:, NG].bitcast(F32), 0.0)
            link(pool.memset(kv_lo[:, NG].bitcast(F32), 0.0))
            pool.sem_inc(consts2_ready, 1)
            split_range(C_KC + 1, C_ADA)
            pool.wait_ge(silu_c_ready, 1)
            for u in range(2):
                pool.wait_ge(bank_full[2 * u + 1], C_ADA // 2)
            for i in range(C_NOUT - C_ADA):
                c = C_ADA + i
                u = c % 2
                pool.wait_ge(raw_landed[u], 16 * (c // 2) + 16 + 96)
                scale = silu_c[:].rearrange("p (k o) -> p k o", o=1).broadcast_to([P, KT, CW])
                link(pool.tensor_tensor(raw[:, u], raw[:, u], scale, ALU.mult))
                link(pool.tensor_tensor(raw[:, u, 0:4], raw[:, u, 0:4], raw[:, u, 4:8], ALU.add))
                link(pool.tensor_tensor(raw[:, u, 0:2], raw[:, u, 0:2], raw[:, u, 2:4], ALU.add))
                link(pool.tensor_tensor(ada_sum[:, i], raw[:, u, 0], raw[:, u, 1], ALU.add))
                pool.sem_inc(lo_done, 1)
            pool.sem_inc(ada_summed, 1)
            split_range(C_NOUT, C_H + 1)
            pool.wait_ge(x_updated, 2 * KT)
            link(pool.memset(minus[:], -1.0))
            link(pool.affine_select(out=tri[:], in_=minus[:], compare_op=ALU.is_ge, fill=0.0, base=0,
                                    pattern=[[-1, P]], channel_multiplier=1))
            pool.tensor_copy(identb3[:], ident[:])
            link(pool.memset(w_z[:, 0], 0.0))
            link(pool.affine_select(out=w_z[:, 0], in_=w_z[:, 0], compare_op=ALU.is_gt, fill=NEG, base=0,
                                    pattern=[[1, P]], channel_multiplier=-1))
            pool.tensor_copy(maskb3[:], w_z[:, 0]).then_inc(consts3_ready, 1)
            split_range(C_H + 1, C_END)

        @block.scalar
        def _(act):
            chained = [0]

            def link(ins):
                chained[0] += 1
                ins.then_inc(act_chain, 1)
                act.wait_ge(act_chain, chained[0])

            more = [0, 0]

            def split_high(c, half, u, first=False):
                if isinstance(c, int) and C_NQ <= c < C_NQ + 4:
                    more[u] += 48
                act.wait_ge(raw_landed[u], 16 * half + 16 + more[u])
                if not first:
                    act.wait_ge(bank_full[2 * u + 1], half)
                act.activation(w_hi[:, u], raw[:, u], ACT.Copy).then_inc(hi_done, 1)

            def stream(c0, n, take, last=False):
                def step(c, half, nhalf, u, j, end=False):
                    if not end:
                        split_high(c + 1, nhalf, 1 - u)
                    for m in range(2):
                        act.wait_ge(bank_full[2 * u + m], half + 1)
                        take(j, m, bank[2 * u + m]).then_inc(bank_free[2 * u + m], 1)
                if n < 4 or last:
                    for j in range(n):
                        c = c0 + j
                        step(c, c // 2, (c + 1) // 2, c % 2, j, end=last and j == n - 1)
                else:
                    with act.Fori(0, n // 2) as i:
                        for v in range(2):
                            c = c0 + v
                            step(2 * i + c, i + c // 2, i + (c + 1) // 2, c % 2, 2 * i + v)

            def ln_and_exp():
                act.preload_act_table_set("natural_log_exp_and_others")

            def norm_front(n):
                for k in range(KT):
                    act.wait_ge(xt_copied if n == 0 else x_updated, k + 1 if n == 0 else KT * (n // 2 - 1) + k + 1)
                    if k >= 2:
                        act.wait_ge(sq_used, KT * n + k - 1)
                    act.activation(tmp[:, k % 2], xT[:, k], ACT.Square).then_inc(sq_ready, 1)

            def root(n):
                ln_and_exp()
                act.wait_ge(sq_used, KT * (n + 1))
                link(act.activation(rstd[:], bank[4][:], ACT.Ln, scale=1.0 / D, bias=eps_col[:]))
                act.activation(rstd[:], rstd[:], ACT.Exp, scale=-0.5).then_inc(rstd_ready, 1)

            def high_parts(n, hi=act_hi, tiles=range(KT)):
                for k in tiles:
                    act.wait_ge(scaled, KT * n + k + 1)
                    act.activation(hi[:, k], tmp[:, k % 2], ACT.Copy).then_inc(act_hi_done, 1)

            def step2(c, take, ahead=True):
                if ahead:
                    split_high(c + 1, (c + 1) // 2, (c + 1) % 2)
                u = c % 2
                for m in range(2):
                    act.wait_ge(bank_full[2 * u + m], c // 2 + 1)
                    take(m, bank[2 * u + m]).then_inc(bank_free[2 * u + m], 1)

            def stream_out(c0, n, y, y_sq):
                for j in range(4):
                    def take(m, b):
                        act.activation(y[:, 2 * j + m, :], b, ACT.Copy)
                        return act.activation(y_sq[:, 2 * j + m, :], b, ACT.Square)
                    step2(c0 + j, take, ahead=(j > 0))
                root(n)

            act.wait_ge(consts_ready, 1)
            norm_front(0)
            split_high(0, 0, 0, first=True)
            root(0)
            split_high(1, 0, 1, first=True)
            high_parts(0)

            act.wait_ge(bank_full[1], 1)
            act.activation(glr_t[:], bank[1][0:16, :], ACT.Copy).then_inc(bank_free[1], 1)
            act.sem_inc(bank_free[0], 1)
            stream(C_Q, 2, lambda j, m, b: act.activation(qk[:, 2 * j + m], b[:], ACT.Copy, scale=GDK ** -0.5))
            ln_and_exp()
            for h in range(GH):
                act.wait_ge(nu_ready, h + 1)
                link(act.activation(kd_t[:, h], kd_t[:, h], ACT.Exp))
                act.activation(kd_t[:, h], kd_t[:, h], ACT.Ln, bias=1.0).then_inc(ln_ready, 1)
            stream(C_K, 2, lambda j, m, b: act.activation(qk[:, GH + 2 * j + m], b[:], ACT.Copy))

            def chunk_exps(h):
                act.wait_ge(gsum_ready, h + 1)
                if h >= 2:
                    act.wait_ge(exps_used, h - 1)
                act.activation(exps[:, h % 2, 0], gate_b[:, h], ACT.Exp, scale=-1.0 / GNORM)
                act.activation(exps[:, h % 2, 1], gate_b[:, h], ACT.Exp, scale=1.0 / GNORM)
                act.wait_ge(grow_ready, h + 1)
                act.activation(exps[:, h % 2, 2], kd_t[:, h], ACT.Exp, scale=1.0 / GNORM).then_inc(exps_ready, 1)
            for j in range(4):
                step2(C_V + j, lambda m, b: act.activation(
                    v_tok[:, 2 * m:2 * m + 2, j * CW:(j + 1) * CW], b.rearrange("p (t n) -> p t n", t=2), ACT.Copy))
                chunk_exps(j)
            stream(C_Z, 4, lambda j, m, b: act.activation(silu_z[:, bass.ds(2 * j + m, 1), :], b[:], ACT.Silu))
            for h in range(GH):
                act.wait_ge(kdt_full, h + 1)
                act.activation(kd_tok[:, h], bank[4 + h][:], ACT.Copy).then_inc(kdtok_ready, 1)
            for t in range(2 * GH):
                act.wait_ge(o_full, t + 1)
                if t >= 2:
                    act.wait_ge(osq_used, t - 1)
                act.activation(tmp[:, t % 2], bank[t % 3][:], ACT.Square).then_inc(o_squared, 1)
            act.wait_ge(osq_used, 2 * GH)
            link(act.activation(head_std[0:GH, :], bank[3][0:GH, :], ACT.Ln, scale=1.0 / GDV, bias=eps_col[0:GH, :]))
            act.activation(head_std[0:GH, :], head_std[0:GH, :], ACT.Exp, scale=-0.5).then_inc(orstd_ready, 1)
            split_high(C_GOUT + 1, (C_GOUT + 1) // 2, (C_GOUT + 1) % 2)
            high_parts(1)
            stream_out(C_GOUT, 1, y_t, y_sq)

            norm_front(2)
            root(2)
            split_high(C_KS, C_KS // 2, C_KS % 2)
            high_parts(2)

            def untaken(c, n=1):
                for c in range(c, c + n):
                    split_high(c + 1, (c + 1) // 2, (c + 1) % 2)

            def unused_banks(c):
                act.sem_inc(bank_free[c % 2 * 2], 1)
                act.sem_inc(bank_free[c % 2 * 2 + 1], 1)

            def kv_high(i):
                act.wait_ge(kv_ready, i + 1)
                act.wait_ge(pe_ready, 1)
                act.wait_ge(consts2_ready, 1)
                act.activation(kv_hi[:, 0:NG], kv_full[:], ACT.Copy)
                act.activation(kv_hi[:, NG, 0:CB:2], pe_t[:, i], ACT.Copy).then_inc(kv_hi_done, 1)

            def hidden(i):
                act.wait_ge(hid_bias_ready, i + 1)
                for m in range(2):
                    src = bank[6 + m][:, 0:NG * NCP]
                    if i == 0:
                        act.activation(hid[:, m], src, ACT.Silu, bias=hid_bias[:, m:m + 1]).then_inc(hid_ready, 1)
                    else:
                        act.activation(hid4[:, m].rearrange("p (g h c) -> p g h c", g=NG, h=NHG),
                                       src.rearrange("p (g o c) -> p g o c", g=NG, o=1).broadcast_to([P, NG, NHG, NCP]),
                                       ACT.Silu, bias=hid_bias[:, m:m + 1]).then_inc(hid_ready, 1)

            act.wait_ge(angle_ready, 2)
            act.activation(sinT[:], sinT[:], ACT.Sin, scale=rope_c[:, 1:2]).then_inc(table_ready, 1)
            act.activation(cosT[:], cosT[:], ACT.Sin).then_inc(table_ready, 1)
            untaken(C_KS)
            kv_high(0)
            split_high(C_VC + 1, (C_VC + 1) // 2, (C_VC + 1) % 2)
            for m in range(2):
                u = C_VC % 2
                act.wait_ge(bank_full[2 * u + m], C_VC // 2 + 1)
                if m == 0:
                    act.wait_ge(kv_split, 1)
                for g in range(2):
                    half = bank[2 * u + m][g * NDH:(g + 1) * NDH, :]
                    act.activation(kv_full[0:NDH, 2 * m + g, 0:S], half, ACT.Copy)
                    last = act.activation(kv_full[NDH:P, 2 * m + g, 0:S - 1], half[:, 1:S], ACT.Copy)
                last.then_inc(bank_free[2 * u + m], 1)
            act.wait_ge(bank_free[2 * (C_VC % 2)], C_VC // 2 + 1)
            act.wait_ge(bank_free[2 * (C_VC % 2) + 1], C_VC // 2 + 1)
            act.sem_inc(kv_ready, 1)
            untaken(C_KW)
            for c in (C_CK, C_CK + 1):
                unused_banks(c)
                untaken(c)
            act.wait_ge(bank_full[2 * ((C_CK + 1) % 2) + 1], (C_CK + 1) // 2 + 1)
            kv_high(1)
            hidden(0)
            for c in (C_VS, C_VW):
                step2(c, lambda m, b, w=c - C_VS: act.activation(
                    v_tok2[:, 2 * m:2 * m + 2, w, :], b.rearrange("p (t n) -> p t n", t=2), ACT.Copy))
            for c in (C_CV, C_CV + 1):
                unused_banks(c)
                untaken(c)
            hidden(1)
            untaken(C_GL)
            act.wait_ge(gate_sum, 2)
            act.activation(gates[:], gates[:], ACT.Sigmoid).then_inc(gate_ready, 1)
            untaken(C_NQ, 4)
            for t in range(TT):
                c = C_NZ + t
                if t < 3:
                    split_high(c + 1, (c + 1) // 2, (c + 1) % 2)
                act.wait_ge(c_shifted, t + 1)
                act.activation(csc[:, 1], csc[:, 0], ACT.Exp, scale=NDH ** -0.5).then_inc(c_exp, 1)
                act.wait_ge(c_tfull, t + 1)
                if t:
                    act.wait_ge(c_out, t)
                act.activation(pcT[:].rearrange("p g q -> p (g q)"), bank[6][:], ACT.Copy).then_inc(c_tcopied, 1)
                for m in range(2):
                    b = 2 * (c % 2) + m
                    act.wait_ge(bank_full[b], c // 2 + 1)
                    act.activation(silu_z2[:, 2 * m:2 * m + 2, t * CW:(t + 1) * CW],
                                   bank[b].rearrange("p (t n) -> p t n", t=2), ACT.Silu).then_inc(bank_free[b], 1)
            act.sem_inc(hi_done, 1)

            act.activation(silu_c[:], vec[:, VAT["c"]:VAT["c"] + KT], ACT.Silu).then_inc(silu_c_ready, 1)
            act.sem_inc(hi_done, C_NOUT - C_ADA - 1)

            for n in range(2 * NPAIR + 2):
                if n >= 2:
                    v = n - 2
                    w = (v // 16 + 1) * P
                    act.wait_ge(t_full, v + 1)
                    if v >= 2:
                        act.wait_ge(pv_full, v - 1)
                    act.activation(probT[:, v % 2, 0, 0:w], bank[4][:, 0:w], ACT.Copy).then_inc(t_sel, 1)
                if n < 2 * NPAIR:
                    keys = (n // 16 + 1) * P
                    act.wait_ge(s_max, n + 1)
                    for w in range(2):
                        act.activation(prob[:, n % 3, w, 0:keys], bank[2 * (n % 2) + w][:, 0:keys], ACT.Exp,
                                       bias=wstat[:, n % 4, w, 1:2], scale=NDH ** -0.5,
                                       accum_out=wstat[:, n % 4, w, 2:3]).then_inc(s_exp, 1)
                if n == 2 * MOD_PAIR + 4:
                    for b in range(4):
                        act.sem_inc(bank_free[b], (C_NOUT - C_ADA) // 2)
                    split_high(C_NOUT, C_NOUT // 2, C_NOUT % 2)
            split_high(C_NOUT + 1, (C_NOUT + 1) // 2, (C_NOUT + 1) % 2)
            for k in range(KT):
                act.wait_ge(ot_full, k + 1)
                act.activation(act_hi[:, k], bank[4 + k % 4][:], ACT.Copy).then_inc(ot_high, 1)
            stream_out(C_NOUT, 3, y_t2, y_sq2)

            norm_front(4)
            root(4)
            split_high(C_H + 1, (C_H + 1) // 2, (C_H + 1) % 2)
            high_parts(3)

            def taker(c):
                s, kind = (c - C_H) // 4 % 2, (c - C_H) % 4
                if c >= C_MA:
                    return lambda m, b: act.activation(mix_a[:, 2 * (c - C_MA) + m], b, ACT.Sigmoid)
                return (lambda m, b: act.activation(qh[:, s, m], b, ACT.Copy, scale=NDH ** -0.5),
                        lambda m, b: act.activation(kh[:, s, m], b, ACT.Copy),
                        lambda m, b: act.activation(vh[:, s, 2 * m:2 * m + 2], b.rearrange("p (t n) -> p t n", t=2), ACT.Copy),
                        lambda m, b: act.activation(zh[:, s, m], b, ACT.Silu))[kind]

            def take3(c, m):
                b = 2 * (c % 2) + m
                act.wait_ge(bank_full[b], c // 2 + 1)
                taker(c)(m, bank[b]).then_inc(bank_free[b], 1)

            def pair_split(p):
                act.wait_ge(head_gated, 2 * p + 2)
                act.activation(br_hi[:, p], gated[:, p % 2], ACT.Copy).then_inc(pair_high, 1)

            for c in range(C_H, C_H + 4):
                step2(c, taker(c), ahead=(c > C_H))
            for h in range(HH):
                c = C_H + 4 + h
                split_high(c + 1, (c + 1) // 2, (c + 1) % 2)
                for i, st in enumerate(range(TT - 1, -1, -1)):
                    act.wait_ge(zc_ready, TT * h + i + 1)
                    act.activation(blocks(ln_z, st), blocks(ln_z, st), ACT.Exp).then_inc(e_ready, 1)
                for i, st in enumerate(range(TT - 1, -1, -1)):
                    act.wait_ge(e_ready, TT * h + i + 1)
                    act.activation(blocks(ln_z, st), blocks(ln_z, st), ACT.Ln, bias=1.0).then_inc(l_ready, 1)
                take3(c, 0)
                if h % 2 == 0 and h:
                    pair_split(h // 2 - 1)
                for i, st in enumerate(range(TT - 1, -1, -1)):
                    act.wait_ge(tri_full, TT * h + i + 1)
                    if h:
                        act.wait_ge(hv_full, h)
                    act.activation(blocks(w_z, st), bank[4 + st][:, st * P:S], ACT.Exp).then_inc(w_ready, 1)
                take3(c, 1)
            pair_split(HH // 2 - 1)
            for c in range(C_U, C_U + 4):
                split_high(c + 1, (c + 1) // 2, (c + 1) % 2)
            for c in range(C_BA, C_BA + 4):
                split_high(c + 1, (c + 1) // 2, (c + 1) % 2)
            stream(C_ZB, 4, lambda j, m, b: act.activation(silu_zb[:, bass.ds(2 * j + m, 1), :], b, ACT.Silu))
            stream(C_MB, 4, lambda j, m, b: act.activation(mix_b[:, bass.ds(2 * j + m, 1), :], b, ACT.Sigmoid))
            for k in range(KT):
                act.wait_ge(d_ready, k // 2 + 1)
                act.activation(act_hi[:, k], pool_u[:, k], ACT.Copy).then_inc(d_high, 1)
            unused_banks(C_MIX)
            split_high(C_MIX + 1, (C_MIX + 1) // 2, (C_MIX + 1) % 2)
            high_parts(4, br_hi)
            for c in range(C_BB, C_BB + 4):
                split_high(c + 1, (c + 1) // 2, (c + 1) % 2)
                high_parts(5, act_hi, range(2 * (c - C_BB), 2 * (c - C_BB) + 2))
            for c in range(C_OUT, C_END):
                if c + 1 < C_END:
                    split_high(c + 1, (c + 1) // 2, (c + 1) % 2)
            for k in range(KT):
                act.wait_ge(x_final, k + 1)
                if k >= 2:
                    act.wait_ge(sq_used, KT * 5 + k - 1)
                act.activation(tmp[:, k % 2], xT[:, k], ACT.Square).then_inc(sq_ready, 1)
            root(5)
            for t in range(TT):
                act.wait_ge(out_full, 2 * t + 1)
                act.activation(out_tok[:, t, 0:S], bank[2 * (t % 2)], ACT.Copy).then_inc(out_left, 1)

        @block.tensor
        def _(pe):
            def arriving(c, ready, at, source=(act_hi, act_lo)):
                x_hi, x_lo = source
                u = c % 2
                pe.wait_ge(lo_done, c + 1)
                for m in range(2):
                    pe.wait_ge(bank_free[2 * u + m], c // 2)
                for k in range(KT):
                    pe.wait_ge(ready, at + k + 1)
                    for m in range(2):
                        for n, (w, x) in enumerate(((w_hi, x_hi), (w_lo, x_hi), (w_hi, x_lo))):
                            mm = pe.matmul(bank[2 * u + m], w[:, u, k, m * P:(m + 1) * P], x[:, k, :],
                                           start=(k == 0 and n == 0), stop=(k == KT - 1 and n == 2))
                        if k == KT - 1:
                            mm.then_inc(bank_full[2 * u + m], 1)

            def product(c, half, u, by_tokens=False, first=False, width=CW, between=None,
                        source=(act_hi, act_lo)):
                x_hi, x_lo = source
                pe.wait_ge(lo_done, c + 1)
                for m in range(2):
                    if not first:
                        pe.wait_ge(bank_free[2 * u + m], half)
                    b = bank[2 * u + m]
                    if by_tokens:
                        for t in range(2):
                            tok = slice((2 * m + t) * P, (2 * m + t + 1) * P)
                            for k in range(KT):
                                for n, (x, w) in enumerate(((x_hi, w_hi), (x_hi, w_lo), (x_lo, w_hi))):
                                    mm = pe.matmul(b[:, t * CW:t * CW + width], x[:, k, tok], w[:, u, k, 0:width],
                                                   start=(k == 0 and n == 0), stop=(k == KT - 1 and n == 2))
                    else:
                        for k in range(KT):
                            for n, (w, x) in enumerate(((w_hi, x_hi), (w_lo, x_hi), (w_hi, x_lo))):
                                mm = pe.matmul(b[:], w[:, u, k, m * P:(m + 1) * P], x[:, k, :],
                                               start=(k == 0 and n == 0), stop=(k == KT - 1 and n == 2))
                    mm.then_inc(bank_full[2 * u + m], 1)
                    if m == 0 and between is not None:
                        between()

            def stream(c0, n, **kw):
                if n < 4:
                    for c in range(c0, c0 + n):
                        product(c, c // 2, c % 2, first=(c < 2), **kw)
                else:
                    with pe.Fori(0, n // 2) as i:
                        for v in range(2):
                            c = c0 + v
                            product(2 * i + c, i + c // 2, c % 2, **kw)

            def mean_square(n, squares):
                for k in range(KT):
                    x = squares(k)
                    pe.matmul(bank[4][:], ones[:], x, start=(k == 0), stop=(k == KT - 1)).then_inc(sq_used, 1)

            def out_product(c0, ready, at, squares):
                def sums(j):
                    for k in (2 * j, 2 * j + 1):
                        c = c0 + j
                        pe.wait_ge(bank_free[2 * (c % 2) + k % 2], c // 2 + 1)
                        pe.matmul(bank[4][:], ones[:], squares[:, k], start=(k == 0), stop=(k == KT - 1)).then_inc(sq_used, 1)
                arriving(c0, ready, at)
                for j in range(1, 4):
                    product(c0 + j, (c0 + j) // 2, (c0 + j) % 2, between=lambda: sums(j - 1))
                sums(3)

            def ring_squares(n):
                def at(k):
                    pe.wait_ge(sq_ready, KT * (n // 2) + k + 1)
                    return tmp[:, k % 2]
                return at

            pe.wait_ge(consts_ready, 1)
            pe.wait_ge(x_landed, 16)
            for k in range(KT):
                if k >= 4:
                    pe.wait_ge(xt_copied, k - 3)
                for t in range(TT):
                    mm = pe.transpose(bank[4 + k % 4][:, t * P:(t + 1) * P], x_tok[:, t, k * P:(k + 1) * P], ident[:])
                mm.then_inc(xt_full, 1)
            pe.wait_ge(vec_landed, 16 * len(VECS))
            pe.transpose(bank[0][:, 0:NVEC], vec_rows[0:NVEC, :], ident[0:NVEC, 0:NVEC]).then_inc(vec_full, 1)
            pe.wait_ge(xt_copied, KT)
            mean_square(0, ring_squares(0))
            pe.wait_ge(vec_ready, 1)

            pe.wait_ge(lo_done, 1)
            for k in range(KT):
                pe.wait_ge(h_ready, k + 1)
                for n, (w, x) in enumerate(((w_hi, act_hi), (w_lo, act_hi), (w_hi, act_lo))):
                    mm = pe.matmul(bank[1][:], w[:, 0, k, 0:P], x[:, k, :],
                                   start=(k == 0 and n == 0), stop=(k == KT - 1 and n == 2))
            mm.then_inc(bank_full[1], 1)
            pe.sem_inc(bank_full[0], 1)
            stream(C_Q, 1)
            pe.wait_ge(bank_free[1], 1)
            pe.wait_ge(up_landed, 16)
            pe.wait_ge(rstd_ready, 1)
            for h in range(GH):
                pe.matmul(bank[4 + h][:], w_up[:, h * P:(h + 1) * P], glr_t[:], start=True, stop=True).then_inc(up_full, 1)
            stream(C_Q + 1, 1)
            stream(C_K, 2)
            stream(C_V, 4, by_tokens=True)
            stream(C_Z, 4)

            for h in range(GH):
                pe.wait_ge(nu_ready, h + 1)
                pe.wait_ge(kd_ready, h + 1)
                for t in range(TT):
                    mm = pe.transpose(bank[4 + h][:, t * P:(t + 1) * P], kd_t[:, h, t * P:(t + 1) * P], ident[:])
                mm.then_inc(kdt_full, 1)
            banks_free(pe, C_GOUT)
            for h in range(GH):
                pe.wait_ge(exps_used, h + 1)
                for t in range(TT):
                    tok = slice(t * P, (t + 1) * P)
                    mm = pe.matmul(bank[h][:, tok], qk[:, GH + h, tok], qk[:, h, tok], start=True, stop=True)
                mm.then_inc(att_full, 1)

            def updates(h):
                pe.wait_ge(kdtok_ready, GH if h == 0 else h + 1)
                if h:
                    pe.wait_ge(upd_read, h)
                for n in range(GN - 1):
                    r = slice(n % 2 * GC, n % 2 * GC + GC)
                    mm = pe.matmul(update_at(n), kd_tok[r, h, n // 2, :],
                                   v_tok[r, n // 2, h * GDV:(h + 1) * GDV], start=True, stop=True)
                mm.then_inc(upd_full, 1)

            def out_squares(t):
                h = t // 2
                pe.wait_ge(o_squared, t + 1)
                pe.matmul(bank[3][0:GH, :], head_sel[:, GH - 1 - h:2 * GH - 1 - h], tmp[:, t % 2],
                          start=(t == 0), stop=(t == 2 * GH - 1)).then_inc(osq_used, 1)

            updates(0)
            pe.wait_ge(att_ready, GH)
            for h in range(GH):
                if h < GH - 1:
                    updates(h + 1)
                for e in range(2):
                    t = 2 * h + e
                    if t >= 3:
                        pe.wait_ge(o_read, t - 2)
                    b = bank[t % 3]
                    ch = slice(h * GDV + e * P, h * GDV + (e + 1) * P)
                    for tt in range(TT):
                        tok = slice(tt * P, (tt + 1) * P)
                        mm = pe.matmul(b[:, tok], v_tok[:, tt, ch], att[:, h, tok], start=True, stop=False)
                        for n in range(2 * tt, 2 * tt + 2):
                            if n:
                                if e == 0:
                                    pe.wait_ge(state_ready, (GN - 1) * h + n)
                                q = slice(n * GC, (n + 1) * GC)
                                mm = pe.matmul(b[:, q], states[:, h % 2, n, e * P:(e + 1) * P], qk[:, h, q],
                                               start=False, stop=(n % 2 == 1))
                    mm.then_inc(o_full, 1)
                    if t:
                        out_squares(t - 1)
            out_squares(2 * GH - 1)
            pe.wait_ge(orstd_ready, 1)
            pe.wait_ge(upd_read, GH)
            for h in range(GH):
                pe.matmul(bank[4 + h][:], ident[0:GH, h:h + 1].broadcast_to([GH, P]), head_std[0:GH, :],
                          start=True, stop=True).then_inc(obc_full, 1)
            out_product(C_GOUT, h_ready, KT, y_sq)

            pe.wait_ge(rstd_ready, 2)
            mean_square(2, ring_squares(2))
            pe.wait_ge(small2_landed, 16 * N_SMALL2)
            pe.transpose(bank[5][:, 0:CB], pe_rows, ident[0:CB, 0:CB]).then_inc(pe_full, 1)

            def turn(r0):
                for r in (r0, r0 + 1):
                    pe.wait_ge(turn_ready, r + 1)
                    if r >= 2:
                        pe.wait_ge(turned, r - 1)
                    else:
                        pe.wait_ge(pe_ready, 1)
                        pe.wait_ge(consts2_ready, 1)
                    pe.matmul(bank[4 + r % 2][:], perm[:], rope_b[:, r % 2], start=True, stop=True).then_inc(turn_full, 1)

            def compress(c, part, i, between=None):
                pe.wait_ge(lo_done, c + 1)
                if part == 0:
                    pe.wait_ge(kv_split, i + 1)
                    if i:
                        pe.wait_ge(cmp_ready, 1)
                    else:
                        pe.wait_ge(consts2_ready, 1)
                u = c % 2
                for m in range(2):
                    for k in range(KT):
                        at = 2 * (KT * part + k)
                        for n, (w, x) in enumerate(((w_hi, kv_hi), (w_lo, kv_hi), (w_hi, kv_lo))):
                            mm = pe.matmul(bank[6 + m][:, 0:(NG + 1) * NCP].rearrange("p (g c) -> p g c", c=NCP),
                                           w[:, u, k, m * P:(m + 1) * P],
                                           x[:, :, at:at + CS * (NCP - 1) + 1:CS],
                                           start=(part == 0 and k == 0 and n == 0),
                                           stop=(part == 1 and k == KT - 1 and n == 2))
                    if m == 0 and between is not None:
                        between()
                mm.then_inc(bank_full[2 * u + 1], 1)
                pe.sem_inc(bank_full[2 * u], 1)

            arriving(C_KC, h_ready, 2 * KT)
            product(C_KS, C_KS // 2, C_KS % 2)
            product(C_VC, C_VC // 2, C_VC % 2, between=lambda: turn(0))
            product(C_KW, C_KW // 2, C_KW % 2, between=lambda: turn(2))
            compress(C_CK, 0, 0, between=lambda: turn(4))
            compress(C_CK + 1, 1, 0)
            product(C_VS, C_VS // 2, C_VS % 2, by_tokens=True)
            pe.wait_ge(hid_ready, 2)
            for m in range(2):
                for half in range(2):
                    mm = pe.matmul(bank[6][half * NDH:(half + 1) * NDH, 0:NG * NCP], w2k[:, m, :], hid[:, m, :],
                                   start=(m == 0), stop=(m == 1))
            mm.then_inc(cmp_full, 1)
            product(C_VW, C_VW // 2, C_VW % 2, by_tokens=True)
            compress(C_CV, 0, 1)
            compress(C_CV + 1, 1, 1)
            product(C_GL, C_GL // 2, C_GL % 2, by_tokens=True, width=48)
            product(C_NQ, C_NQ // 2, C_NQ % 2)
            pe.wait_ge(hid_ready, 4)
            for g in range(NG):
                for m in range(2):
                    mm = pe.matmul(bank[6][:, g * NDH:(g + 1) * NDH],
                                   hid4[:, m, g * P:(g + 1) * P],
                                   w2v[:, m, :], start=(m == 0), stop=(m == 1))
            mm.then_inc(cmp_full, 1)
            for j in range(1, 4):
                product(C_NQ + j, (C_NQ + j) // 2, (C_NQ + j) % 2, between=lambda: turn(4 + 2 * j))
            pe.wait_ge(turn_ready, 14)
            turn(12)

            def scores(p):
                t, i = p // 8, p % 8
                tok = slice(t * P, (t + 1) * P)
                g = i // 4
                if p:
                    pe.wait_ge(s_exp, 4 * p)
                for kT in (ksT, kwT):
                    for half in range(2):
                        rows = slice(half * NDH, (half + 1) * NDH)
                        b = bank[2 * half + (kT is kwT)]
                        pe.matmul(b[:, 0:(t + 1) * P], qT[rows, i, tok], kT[rows, g, 0:(t + 1) * P], start=True, stop=False)
                for half in range(2):
                    for w in range(2):
                        mm = pe.matmul(bank[2 * half + w][:, t * P:(t + 1) * P], identb[:], maskb[:], start=False, stop=True)
                    mm.then_inc(s_full, 1)

            def turn_weights(n):
                t = n // 16
                pe.wait_ge(s_exp, 2 * (n + 1))
                if n:
                    pe.wait_ge(t_sel, n)
                    pe.wait_ge(t_win, n)
                for w in range(2):
                    for k in range(t + 1):
                        mm = pe.transpose(bank[4 + w][:, k * P:(k + 1) * P], prob[:, n % 3, w, k * P:(k + 1) * P], ident[:])
                mm.then_inc(t_full, 1)

            def values(n):
                t, i, half = n // 16, n % 16 // 2, n % 2
                g = 2 * (i // 4) + half
                pe.wait_ge(t_sel, n + 1)
                pe.wait_ge(t_win, n + 1)
                if n >= 2:
                    pe.wait_ge(pv_read, n - 1)
                for w in range(2):
                    for k in range(t + 1):
                        mm = pe.matmul(bank[6 + n % 2][:, w * NDH:(w + 1) * NDH], probT[:, n % 2, w, k * P:(k + 1) * P],
                                       v_tok2[:, k, w, g * NDH:(g + 1) * NDH], start=(k == 0), stop=(k == t))
                mm.then_inc(pv_full, 1)

            def modulation():
                pe.wait_ge(ada_summed, 1)
                for i in range(3 * KT):
                    mm = pe.matmul(bank[7][:, i:i + 1], ada_sum[:, i // 2, i % 2 * P:(i % 2 + 1) * P], ones[:, 0:1],
                                   start=True, stop=True)
                mm.then_inc(mod_full, 1)
                pe.wait_ge(mod_full, 1)
                for b in range(4):
                    pe.sem_inc(bank_full[b], (C_NOUT - C_ADA) // 2)

            def c_score(t):
                tok = slice(t * P, (t + 1) * P)
                if t == 0:
                    pe.wait_ge(turned, 14)
                    pe.wait_ge(cmp_ready, 2)
                for i in range(8):
                    for half in range(2):
                        rows = slice(half * NDH, (half + 1) * NDH)
                        g = 2 * (i // 4) + half
                        mm = pe.matmul(bank[4 + half][:, i * NCP:(i + 1) * NCP], qT[rows, i, tok],
                                       kcmpT[rows, g * NCP:(g + 1) * NCP], start=True, stop=True)
                mm.then_inc(c_scores, 1)

            def c_turn(t):
                pe.wait_ge(c_prob, t + 1)
                if t:
                    pe.wait_ge(c_taken, t)
                for g in range(NG):
                    pc = csc[:, 1].rearrange("p (h i c) -> p h i c", h=2, i=8)[:, g % 2, g // 2 * 4:g // 2 * 4 + 4, :]
                    mm = pe.transpose(bank[6][:, g * P:(g + 1) * P], pc.rearrange("p i c -> p (i c)"), ident[:])
                mm.then_inc(c_tfull, 1)

            def c_values(t):
                pe.wait_ge(c_tcopied, t + 1)
                for g in range(NG):
                    mm = pe.matmul(bank[6 + g // 2][:, g % 2 * CW:(g % 2 + 1) * CW], pcT[:, g, :], vcmp[:, g, :],
                                   start=True, stop=True)
                mm.then_inc(c_out, 1)

            for t in range(TT):
                c_score(t)
                c = C_NZ + t
                product(c, c // 2, c % 2, by_tokens=True, between=lambda: c_turn(t))
                c_values(t)
            banks_free(pe, C_ADA)
            pe.wait_ge(c_taken, TT)
            scores(0)
            for p in range(NPAIR):
                turn_weights(2 * p)
                if p:
                    values(2 * p - 1)
                if p < NPAIR - 1:
                    scores(p + 1)
                turn_weights(2 * p + 1)
                if p == MOD_PAIR:
                    pe.wait_ge(pv_read, 2 * p)
                    modulation()
                values(2 * p)
                if p == MOD_PAIR:
                    pe.wait_ge(mod_ready, 1)
            values(2 * NPAIR - 1)
            pe.wait_ge(o_gated, TT)
            for k in range(KT):
                if k >= 4:
                    pe.wait_ge(ot_low, k - 3)
                for t in range(TT):
                    mm = pe.transpose(bank[4 + k % 4][:, t * P:(t + 1) * P], o_tok[:, t, k * P:(k + 1) * P], ident[:])
                mm.then_inc(ot_full, 1)
            out_product(C_NOUT, ot_low, 0, y_sq2)


            pe.wait_ge(rstd_ready, 4)
            mean_square(4, ring_squares(4))
            arriving(C_H, h_ready, 3 * KT)
            for c in range(C_H + 1, C_H + 4):
                product(c, c // 2, c % 2, by_tokens=(c == C_H + 2))

            def rows3(h):
                return slice(h % 2 * NDH, (h % 2 + 1) * NDH)

            def head_scores(h):
                s, tile = h // 4 % 2, h % 4 // 2
                for st in range(TT - 1, -1, -1):
                    if h:
                        pe.wait_ge(w_ready, TT * (h - 1) + TT - st)
                        if st == 0:
                            pe.wait_ge(head_gated, h)
                    b = bank[4 + st]
                    pe.matmul(b[:, st * P:S], kh[rows3(h), s, tile, st * P:(st + 1) * P], qh[rows3(h), s, tile, st * P:S],
                              start=True, stop=False)
                    pe.matmul(b[:, st * P:(st + 1) * P], identb3[:], maskb3[:], start=False, stop=True)\
                        .then_inc(z_full, 1)

            def head_sums(h):
                for i, st in enumerate(range(TT - 1, -1, -1)):
                    pe.wait_ge(sp_ready, TT * h + i + 1)
                    for jt in range(TT - 1, st - 1, -1):
                        mm = pe.matmul(bank[4 + st][:, jt * P:S], (tri if jt == st else minus)[:], blocks(sp_z, jt),
                                       start=False, stop=(jt == st), skip_group_check=True)
                    mm.then_inc(tri_full, 1)

            def head_values(h):
                s = h // 4 % 2
                pe.wait_ge(w_ready, TT * (h + 1))
                for st in range(TT):
                    mm = pe.matmul(bank[4][rows3(h), st * P:S], vh[:, s, st, h % 4 * NDH:(h % 4 + 1) * NDH], blocks(w_z, st),
                                   start=(st == 0), stop=(st == TT - 1))
                mm.then_inc(hv_full, 1)

            pe.wait_ge(consts3_ready, 1)
            banks_free(pe, C_H + 4)
            for h in range(HH):
                c = C_H + 4 + h
                head_scores(h)
                product(c, c // 2, c % 2, by_tokens=(c < C_MA and h % 4 == 2), between=lambda: head_sums(h))
                head_values(h)
            stream(C_U, 4)
            pe.wait_ge(pair_low, KT)
            stream(C_BA, 4, source=(br_hi, br_lo))
            stream(C_ZB, 4)
            stream(C_MB, 4)
            c, u = C_MIX, C_MIX % 2
            pe.wait_ge(lo_done, c + 1)
            pe.wait_ge(d_low, KT)
            pe.wait_ge(head_gated, HH)
            for tile in range(KT):
                if tile >= 4:
                    pe.wait_ge(mix_taken, tile - 3)
                for i in range(2):
                    k = tile // 2 * 2 + i
                    for n, (w, x) in enumerate(((w_hi, act_hi), (w_lo, act_hi), (w_hi, act_lo))):
                        mm = pe.matmul(bank[4 + tile % 4], w[:, u, k, tile % 2 * P:(tile % 2 + 1) * P], x[:, k, :],
                                       start=(i == 0 and n == 0), stop=(i == 1 and n == 2))
                mm.then_inc(mix_full if tile < KT - 1 else bank_full[2 * u + 1], 1)
            pe.sem_inc(bank_full[2 * u], 1)
            arriving(C_BB, h_ready, 4 * KT, source=(br_hi, br_lo))
            for c in range(C_BB + 1, C_BB + 4):
                product(c, c // 2, c % 2, source=(br_hi, br_lo))
            arriving(C_OUT, h_ready, 5 * KT)
            for c in range(C_OUT + 1, C_OUT + 4):
                product(c, c // 2, c % 2)
            pe.wait_ge(mix_taken, KT)
            def final_squares(k):
                pe.wait_ge(sq_ready, KT * 3 + k + 1)
                return tmp[:, k % 2]
            mean_square(5, final_squares)
            pe.wait_ge(fin_ready, KT)
            for t in range(TT):
                if t >= 2:
                    pe.wait_ge(out_left, t - 1)
                    pe.wait_ge(out_right, t - 1)
                for g in range(2):
                    for k in range(4):
                        mm = pe.transpose(bank[2 * (t % 2) + g][:, k * P:(k + 1) * P],
                                          xT[:, 4 * g + k, t * P:(t + 1) * P], ident[:])
                    mm.then_inc(out_full, 1)

        @block.vector
        def _(dve):
            chained = [0]

            def link(ins):
                chained[0] += 1
                ins.then_inc(dve_chain, 1)
                dve.wait_ge(dve_chain, chained[0])

            def inverse_root(n):
                dve.wait_ge(rstd_ready, n + 1)

            def split_act(n, scale, to=(act_hi, act_lo)):
                hi, lo = to

                def low(k):
                    dve.wait_ge(act_hi_done, KT * n + k + 1)
                    dve.tensor_tensor(lo[:, k], tmp[:, k % 2], hi[:, k].bitcast(F32),
                                      ALU.subtract).then_inc(h_ready, 1)
                for k in range(KT):
                    if k >= 2:
                        dve.wait_ge(h_ready, KT * n + k - 1)
                    scale(k).then_inc(scaled, 1)
                    if k:
                        low(k - 1)
                low(KT - 1)

            for k in range(KT):
                dve.wait_ge(xt_full, k + 1)
                dve.tensor_copy(xT[:, k], bank[4 + k % 4][:]).then_inc(xt_copied, 1)
            dve.wait_ge(vec_full, 1)
            dve.tensor_copy(vec[:], bank[0][:, 0:NVEC]).then_inc(vec_ready, 1)
            dve.wait_ge(vec_ready, 1)
            dve.tensor_scalar(neg_bgk[:], vec[:, VAT["b_gk"]:VAT["b_gk"] + GH], -1.0, None, ALU.mult)
            inverse_root(0)
            split_act(0, lambda k: dve.scalar_tensor_tensor(tmp[:, k % 2], xT[:, k], vcol("pre0", k), rstd[:],
                                                            ALU.mult, ALU.mult))
            for h in range(GH):
                dve.wait_ge(up_full, h + 1)
                link(dve.tensor_scalar(gate_b[:, h], bank[4 + h][:], -1.0, neg_bgk[:, h:h + 1], ALU.mult, ALU.add))
                dve.tensor_scalar(kd_t[:, h], gate_b[:, h], CAP, None, ALU.min).then_inc(nu_ready, 1)
            for h in range(GH):
                g = gate_b[:, h].rearrange("p (n c) -> p n c", c=GC)
                dve.wait_ge(ln_ready, h + 1)
                link(dve.tensor_tensor(gate_b[:, h], kd_t[:, h], gate_b[:, h], ALU.max))
                dve.tensor_tensor_scan(gate_b[:, h], chunk_keep[:], gate_b[:, h], 0.0, ALU.mult,
                                       ALU.add).then_inc(gsum_ready, 1)
                dve.wait_ge(gsum_ready, h + 1)
                dve.tensor_tensor(kd_t[:, h].rearrange("p (n c) -> p n c", c=GC), g,
                                  g[:, :, GC - 1:GC].broadcast_to([P, GN, GC]), ALU.subtract).then_inc(grow_ready, 1)
            for h in range(GH):
                dve.wait_ge(exps_ready, h + 1)
                if h == 0:
                    banks_free(dve, C_K + 2)
                e = exps[:, h % 2]
                dve.tensor_tensor(qk[:, h], qk[:, h], e[:, 0], ALU.mult)
                dve.tensor_copy(decay[:, h].rearrange("p (n o) -> p n o", o=1),
                                e[:, 0].rearrange("p (n c) -> p n c", c=GC)[:, :, GC - 1:GC])
                link(dve.tensor_tensor(kd_t[:, h], qk[:, GH + h], e[:, 2], ALU.mult))
                dve.sem_inc(kd_ready, 1)
                dve.tensor_tensor(qk[:, GH + h], qk[:, GH + h], e[:, 1], ALU.mult).then_inc(exps_used, 1)
            for h in range(GH):
                dve.wait_ge(att_full, h + 1)
                dve.copy_predicated(att[:, h].rearrange("p (t i) -> p t i", i=P),
                                    causal[:].rearrange("p (o i) -> p o i", o=1).broadcast_to([P, TT, P]),
                                    bank[h][:].rearrange("p (t i) -> p t i", i=P)).then_inc(att_ready, 1)
            def take_out(t):
                dve.wait_ge(o_squared, t + 1)
                dve.scalar_tensor_tensor(o_t[:, t], bank[t % 3][:], vcol("head_norm", t % 2), silu_z[:, t],
                                         ALU.mult, ALU.mult).then_inc(o_read, 1)
            for h in range(GH):
                dve.wait_ge(upd_full, h + 1)
                if h >= 2:
                    dve.wait_ge(o_full, 2 * (h - 1))
                for n in range(1, GN):
                    upd = update_at(n - 1)
                    if n == 1:
                        dve.tensor_copy(states[:, h % 2, n], upd).then_inc(state_ready, 1)
                    else:
                        dve.wait_ge(state_ready, (GN - 1) * h + n - 1)
                        dve.scalar_tensor_tensor(states[:, h % 2, n], states[:, h % 2, n - 1], decay[:, h, n - 1:n], upd,
                                                 ALU.mult, ALU.add).then_inc(state_ready, 1)
                dve.wait_ge(state_ready, (GN - 1) * (h + 1))
                dve.sem_inc(upd_read, 1)
                if h:
                    take_out(2 * h - 2)
                    take_out(2 * h - 1)
            take_out(2 * GH - 2)
            take_out(2 * GH - 1)
            dve.wait_ge(obc_full, GH)
            dve.wait_ge(osq_used, 2 * GH)
            dve.wait_ge(o_read, 2 * GH)
            split_act(1, lambda k: dve.tensor_tensor(tmp[:, k % 2], o_t[:, k], bank[4 + k // 2][:], ALU.mult))

            def residual(n, name, y):
                inverse_root(n)
                for k in range(KT):
                    link(dve.scalar_tensor_tensor(y[:, k], y[:, k], vcol(name, k), rstd[:], ALU.mult, ALU.mult))
                    dve.tensor_tensor(xT[:, k], xT[:, k], y[:, k], ALU.add).then_inc(x_updated, 1)
            residual(1, "post0", y_t)

            inverse_root(2)
            dve.wait_ge(pe_full, 1)
            dve.tensor_copy(pe_t[:].rearrange("p i m -> p (i m)"), bank[5][:, 0:CB]).then_inc(pe_ready, 1)
            split_act(2, lambda k: dve.scalar_tensor_tensor(tmp[:, k % 2], xT[:, k], vcol("pre1", k), rstd[:],
                                                            ALU.mult, ALU.mult))

            dve.wait_ge(small2_landed, 16 * N_SMALL2)
            pos, turns = rope_a[:, 0], rope_b[:, 0]
            link(dve.tensor_copy(rope_a[:, 1], pos.bitcast(I32)))
            link(dve.tensor_scalar(rope_a[:, 1], rope_a[:, 1], rope_c[:, 0:1], None, ALU.mult))
            for tab, shift in ((sinT, 0.0), (cosT, 0.25)):
                link(dve.tensor_scalar(turns, rope_a[:, 1], 1.0 / (2.0 * np.pi), shift, ALU.mult, ALU.add))
                link(dve.tensor_scalar(turns, turns, ROUND, -ROUND, ALU.add, ALU.add))
                src = rope_a[:, 1]
                for part in TWO_PI:
                    link(dve.scalar_tensor_tensor(tab[:], turns, -part, src, ALU.mult, ALU.add))
                    src = tab[:]
                link(dve.tensor_scalar(tab[:], tab[:], 2.0 * np.pi * shift, PI_DOWN, ALU.add, ALU.min))
                dve.tensor_scalar(tab[:], tab[:], -PI_DOWN, None, ALU.max).then_inc(angle_ready, 1)
            def turn_parts(c, r0):
                for m in range(2):
                    b = 2 * (c % 2) + m
                    dve.wait_ge(bank_full[b], c // 2 + 1)
                    if r0 + m >= 2:
                        dve.wait_ge(turned, r0 + m - 1)
                    dve.tensor_tensor(rope_a[:, m], bank[b][:], cosT[:], ALU.mult)
                    link(dve.tensor_tensor(rope_b[:, m], bank[b][:], sinT[:], ALU.mult))
                    dve.sem_inc(turn_ready, 1)
                    dve.sem_inc(bank_free[b], 1)

            def turn_sum(r0, dst):
                for m in range(2):
                    dve.wait_ge(turn_full, r0 + m + 1)
                    dve.tensor_tensor(dst(m), rope_a[:, m], bank[4 + m][:], ALU.add).then_inc(turned, 1)

            def kv_low(i):
                dve.wait_ge(kv_hi_done, i + 1)
                dve.tensor_tensor(kv_lo[:, 0:NG], kv_full[:], kv_hi[:, 0:NG].bitcast(F32), ALU.subtract)
                dve.tensor_tensor(kv_lo[:, NG, 0:CB:2], pe_t[:, i], kv_hi[:, NG, 0:CB:2].bitcast(F32),
                                  ALU.subtract).then_inc(kv_split, 1)

            def hidden_bias(i):
                for m in range(2):
                    c = (C_CK, C_CV)[i] + 1
                    dve.wait_ge(bank_full[2 * (c % 2) + 1], c // 2 + 1)
                    link(dve.tensor_copy(hid_bias[:, m:m + 1], bank[6 + m][:, NG * NCP:NG * NCP + 1]))
                dve.sem_inc(hid_bias_ready, 1)

            dve.wait_ge(table_ready, 2)
            turn_parts(C_KC, 0)
            for m in range(2):
                dve.wait_ge(turn_full, m + 1)
                for g in range(2):
                    a = rope_a[g * NDH:(g + 1) * NDH, m]
                    b = bank[4 + m][g * NDH:(g + 1) * NDH, :]
                    dve.tensor_tensor(kv_full[0:NDH, 2 * m + g, 0:S], a, b, ALU.add)
                    last = dve.tensor_tensor(kv_full[NDH:P, 2 * m + g, 0:S - 1], a[:, 1:S], b[:, 1:S], ALU.add)
                last.then_inc(turned, 1)
            dve.wait_ge(turned, 2)
            dve.sem_inc(kv_ready, 1)
            turn_parts(C_KS, 2)
            kv_low(0)
            turn_sum(2, lambda m: ksT[:, m])
            turn_parts(C_KW, 4)
            turn_sum(4, lambda m: kwT[:, m])
            hidden_bias(0)
            kv_low(1)
            dve.wait_ge(cmp_full, 1)
            dve.tensor_copy(kcmpT[:], bank[6][:, 0:NG * NCP]).then_inc(cmp_ready, 1)
            hidden_bias(1)
            for m in range(2):
                b = 2 * (C_GL % 2) + m
                dve.wait_ge(bank_full[b], C_GL // 2 + 1)
                link(dve.tensor_tensor(gates[:, 2 * m:2 * m + 2, :],
                                       bank[b][:].rearrange("p (t n) -> p t n", t=2)[:, :, 0:48],
                                       gate_bias[:].rearrange("p (o n) -> p o n", o=1).broadcast_to([P, 2, 48]), ALU.add))
                dve.sem_inc(gate_sum, 1)
                dve.sem_inc(bank_free[b], 1)
            turn_parts(C_NQ, 6)
            dve.wait_ge(cmp_full, 2)
            for h in range(NHG):
                r = slice(h * NCP, (h + 1) * NCP)
                last = dve.tensor_copy(vcmp[r, :, h * NDH:(h + 1) * NDH],
                                       bank[6][r, 0:CW].rearrange("p (g d) -> p g d", g=NG))
            last.then_inc(cmp_ready, 1)
            for j in range(4):
                turn_sum(6 + 2 * j, lambda m: qT[:, 2 * j + m])
                if j < 3:
                    turn_parts(C_NQ + j + 1, 8 + 2 * j)
            dve.wait_ge(gate_ready, 1)

            def compressed(t):
                heads = lambda a: a.rearrange("p (h c) -> p h c", c=NCP)
                over_heads = lambda a, n: a.rearrange("p (o c) -> p o c", o=1).broadcast_to([P, n, NCP])
                over_blocks = lambda a: a.rearrange("p (h o) -> p h o", o=1).broadcast_to([P, 16, NCP])
                dve.wait_ge(c_scores, t + 1)
                if t:
                    dve.wait_ge(c_tfull, t)
                for half in range(2):
                    link(dve.tensor_tensor(heads(csc[:, 0, half * CW:(half + 1) * CW]), heads(bank[4 + half][:, 0:CW]),
                                           over_heads(cmask[:, t], 8), ALU.add))
                link(dve.tensor_reduce(cstat[:, 0], heads(csc[:, 0]), AX_X, ALU.max))
                dve.tensor_tensor(heads(csc[:, 0]), heads(csc[:, 0]), over_blocks(cstat[:, 0]), ALU.subtract).then_inc(c_shifted, 1)
                dve.wait_ge(c_exp, t + 1)
                link(dve.tensor_tensor(heads(csc[:, 1]), heads(csc[:, 1]), over_heads(cvalid[:, t], 16), ALU.mult))
                link(dve.tensor_reduce(cstat[:, 1], heads(csc[:, 1]), AX_X, ALU.add))
                link(dve.tensor_scalar(cstat[:, 1], cstat[:, 1], 1e-30, None, ALU.max))
                link(dve.reciprocal(cstat[:, 1], cstat[:, 1]))
                for half in range(2):
                    g = gates[:, t].rearrange("p (a h j c) -> p a h j c", a=2, h=2, j=4)[:, :, half, :, 0]
                    o = cstat[:, 2, 8 * half:8 * half + 8].rearrange("p (a j) -> p a j", a=2)
                    i = cstat[:, 1, 8 * half:8 * half + 8].rearrange("p (a j) -> p a j", a=2)
                    link(dve.tensor_tensor(o, i, g, ALU.mult))
                dve.tensor_tensor(heads(csc[:, 1]), heads(csc[:, 1]), over_blocks(cstat[:, 2]), ALU.mult).then_inc(c_prob, 1)
                dve.wait_ge(c_out, t + 1)
                for b in range(2):
                    last = dve.tensor_copy(o_tok[:, t, b * 512:(b + 1) * 512], bank[6 + b][:])
                link(last)
                dve.sem_inc(c_taken, 1)

            def unit_max(n):
                t = n // 16
                dve.wait_ge(s_full, n + 1)
                st = wstat[:, n % 4]
                link(dve.tensor_reduce(st[:, :, 0], banks[:, 2 * (n % 2):2 * (n % 2) + 2, 0:(t + 1) * P], AX_X, ALU.max))
                dve.tensor_scalar(st[:, :, 1], st[:, :, 0], -NDH ** -0.5, None, ALU.mult).then_inc(s_max, 1)

            def unit_weights(n):
                t, i, half = n // 16, n % 16 // 2, n % 2
                h = i // 4 * 8 + half * 4 + i % 4
                st = wstat[:, n % 4]
                dve.wait_ge(t_full, n + 1)
                if n >= 2:
                    dve.wait_ge(pv_full, n - 1)
                dve.tensor_copy(probT[:, n % 2, 1, 0:(t + 1) * P], bank[5][:, 0:(t + 1) * P]).then_inc(t_win, 1)
                link(dve.reciprocal(st[:, :, 3], st[:, :, 2]))
                link(dve.tensor_tensor(st[:, :, 3], st[:, :, 3], gates[:, t, 3 * h + 1:3 * h + 3], ALU.mult))

            def unit_out(n):
                t, i, half = n // 16, n % 16 // 2, n % 2
                h = i // 4 * 8 + half * 4 + i % 4
                o = o_tok[:, t, h * NDH:(h + 1) * NDH]
                dve.wait_ge(pv_full, n + 1)
                link(dve.scalar_tensor_tensor(o, bank[6 + n % 2][:, 0:NDH], wstat[:, n % 4, 0, 3:4], o, ALU.mult, ALU.add))
                dve.scalar_tensor_tensor(o, bank[6 + n % 2][:, NDH:2 * NDH], wstat[:, n % 4, 1, 3:4], o,
                                         ALU.mult, ALU.add).then_inc(pv_read, 1)

            for t in range(TT):
                compressed(t)
            for n in range(2 * NPAIR + 3):
                if 2 <= n < 2 * NPAIR + 2:
                    unit_weights(n - 2)
                if n < 2 * NPAIR:
                    unit_max(n)
                if n >= 3:
                    unit_out(n - 3)
                if n >= 3 and (n - 3) % 16 == 15:
                    t = (n - 3) // 16
                    dve.wait_ge(pv_read, 16 * (t + 1))
                    if t == 0:
                        banks_free(dve, C_ADA)
                    dve.tensor_tensor(o_tok[:, t], o_tok[:, t], silu_z2[:, t], ALU.mult).then_inc(o_gated, 1)
                if n == 2 * MOD_PAIR + 2:
                    dve.wait_ge(mod_full, 1)
                    dve.tensor_tensor(mod[:], bank[7][:, 0:3 * KT], vec[:, VAT["b_ada"]:VAT["b_ada"] + 3 * KT],
                                      ALU.add).then_inc(mod_ready, 1)
            for k in range(KT):
                dve.wait_ge(ot_high, k + 1)
                dve.tensor_tensor(act_lo[:, k], bank[4 + k % 4][:], act_hi[:, k].bitcast(F32), ALU.subtract).then_inc(ot_low, 1)
            residual(3, "post1", y_t2)

            dve.wait_ge(mod_ready, 1)
            link(dve.scalar_tensor_tensor(gain_mod[:], mod[:, KT:2 * KT], 1.0, vec[:, VAT["gain2"]:VAT["gain2"] + KT],
                                          ALU.add, ALU.mult))
            inverse_root(4)

            def modulated(k):
                link(dve.scalar_tensor_tensor(tmp[:, k % 2], xT[:, k], gain_mod[:, k:k + 1], rstd[:], ALU.mult, ALU.mult))
                return dve.tensor_scalar(tmp[:, k % 2], tmp[:, k % 2], mod[:, k:k + 1], None, ALU.add)
            split_act(3, modulated)

            def pair_part(p):
                dve.wait_ge(pair_high, p + 1)
                dve.tensor_tensor(br_lo[:, p], gated[:, p % 2], br_hi[:, p].bitcast(F32), ALU.subtract).then_inc(pair_low, 1)

            for h in range(HH):
                r = slice(h % 2 * NDH, (h % 2 + 1) * NDH)
                for i, st in enumerate(range(TT - 1, -1, -1)):
                    dve.wait_ge(z_full, TT * h + i + 1)
                    dve.tensor_scalar(blocks(ln_z, st), bank[4 + st][:, st * P:S], CAP, None, ALU.min).then_inc(zc_ready, 1)
                for i, st in enumerate(range(TT - 1, -1, -1)):
                    dve.wait_ge(l_ready, TT * h + i + 1)
                    if h:
                        dve.wait_ge(tri_full, TT * h)
                    dve.tensor_tensor(blocks(sp_z, st), blocks(ln_z, st), bank[4 + st][:, st * P:S],
                                      ALU.max).then_inc(sp_ready, 1)
                if h % 2 == 0 and h:
                    pair_part(h // 2 - 1)
                dve.wait_ge(hv_full, h + 1)
                dve.tensor_tensor(gated[r, h // 2 % 2], bank[4][r, :], zh[r, h // 4 % 2, h % 4 // 2], ALU.mult)\
                    .then_inc(head_gated, 1)
            pair_part(HH // 2 - 1)

            dve.wait_ge(small3_landed, 16)
            for g, window in enumerate(WINDOWS):
                c = C_U + g
                u = pool_u[:, 2 * g:2 * g + 2]
                for m in range(2):
                    b = 2 * (c % 2) + m
                    dve.wait_ge(bank_full[b], c // 2 + 1)
                    link(dve.tensor_copy(u[:, m], bank[b]))
                    dve.sem_inc(bank_free[b], 1)
                src, step, n = u, 1, 0
                while step < window:
                    dst = sums[n % 2]
                    dve.tensor_copy(dst[:, :, 0:step], src[:, :, 0:step])
                    link(dve.tensor_tensor(dst[:, :, step:S], src[:, :, step:S], src[:, :, 0:S - step], ALU.add))
                    src, step, n = dst, 2 * step, n + 1
                link(dve.tensor_tensor(src[:, :, 0:16], src[:, :, 0:16],
                                       pool_fix[:, g:g + 1].broadcast_to([P, 2, 16]), ALU.mult))
                link(dve.scalar_tensor_tensor(u, src[:], 1.0 / window, u, ALU.mult, ALU.subtract))
                dve.sem_inc(d_ready, 1)
            with dve.Fori(0, 2) as i:
                for v in range(2):
                    c = C_BA + v
                    for m in range(2):
                        b = 2 * (c % 2) + m
                        dve.wait_ge(bank_full[b], i + (c // 2 + 1))
                        part = mix_a[:, bass.ds(4 * i + (2 * v + m), 1), :]
                        dve.tensor_tensor(part, part, bank[b].rearrange("p (o s) -> p o s", o=1), ALU.mult).then_inc(bank_free[b], 1)
            banks_free(dve, C_MIX)
            for k in range(KT):
                dve.wait_ge(d_high, k + 1)
                dve.tensor_tensor(act_lo[:, k], pool_u[:, k], act_hi[:, k].bitcast(F32), ALU.subtract).then_inc(d_low, 1)

            def pooled(k):
                if k < KT - 1:
                    dve.wait_ge(mix_full, k + 1)
                else:
                    dve.wait_ge(bank_full[2 * (C_MIX % 2) + 1], C_MIX // 2 + 1)
                link(dve.scalar_tensor_tensor(tmp[:, k % 2], bank[4 + k % 4], vcol("pool_scale", k), silu_zb[:, k],
                                              ALU.mult, ALU.mult))
                dve.sem_inc(mix_taken, 1)
                return dve.engine_nop()
            split_act(4, pooled, (br_hi, br_lo))

            def merged(k):
                c = C_BB + k // 2
                b = 2 * (c % 2) + k % 2
                dve.wait_ge(bank_full[b], c // 2 + 1)
                link(dve.tensor_tensor(tmp[:, k % 2], bank[b], mix_b[:, k], ALU.mult))
                dve.sem_inc(bank_free[b], 1)
                return dve.tensor_tensor(tmp[:, k % 2], tmp[:, k % 2], mix_a[:, k], ALU.add)
            split_act(5, merged)
            for k in range(KT):
                c = C_OUT + k // 2
                b = 2 * (c % 2) + k % 2
                dve.wait_ge(bank_full[b], c // 2 + 1)
                link(dve.scalar_tensor_tensor(xT[:, k], bank[b], mod[:, 2 * KT + k:2 * KT + k + 1], xT[:, k],
                                              ALU.mult, ALU.add))
                dve.sem_inc(x_final, 1)
                dve.sem_inc(bank_free[b], 1)
            inverse_root(5)
            for k in range(KT):
                dve.scalar_tensor_tensor(xT[:, k], xT[:, k], vcol("final", k), rstd[:], ALU.mult, ALU.mult).then_inc(fin_ready, 1)
            for t in range(TT):
                dve.wait_ge(out_full, 2 * t + 2)
                dve.tensor_copy(out_tok[:, t, S:D], bank[2 * (t % 2) + 1]).then_inc(out_right, 1)


_INS = ["x", "positions", "pre_norm", "post_norm", "gla_w_in", "gla_w_gk_up", "gla_b_gk", "gla_head_norm", "gla_w_out",
        "nsa_w_in", "nsa_b_gate", "nsa_pe_k", "nsa_pe_v", "nsa_ck_w1", "nsa_ck_w2", "nsa_cv_w1", "nsa_cv_w2",
        "nsa_w_out", "c_2", "norm_gain_2", "w_ada_2", "b_ada_2", "w_in_2", "pool_w_2", "pool_scale_2",
        "w_branch_a_2", "w_branch_b_2", "w_out_2", "final_gain_2"]


def named(aps):
    A = {}
    for name, a in aps.items():
        if a.shape[0] == 1:
            a = a[0]
        A[name] = a
    A["pre0"], A["pre1"], A["post0"], A["post1"] = (aps["pre_norm"][0], aps["pre_norm"][1], aps["post_norm"][0],
                                                    aps["post_norm"][1])
    A["gain2"], A["final"], A["b_ada"], A["pool_scale"] = (A["norm_gain_2"], A["final_gain_2"], A["b_ada_2"],
                                                           A["pool_scale_2"])
    A["pool_w_2"] = A["pool_w_2"].rearrange("g c d -> (g c) d")
    A["c"], A["b_gk"], A["head_norm"] = A["c_2"], A["gla_b_gk"], A["gla_head_norm"]
    return A


def shape_constants():
    half = NDH // 2
    inv = 10000.0 ** (-np.arange(0, NDH, 2, dtype=np.float64) / NDH)
    sign = np.where(np.arange(P) % NDH < half, 1.0, -1.0)
    t = np.arange(1, 17)
    return {"rope_const": np.stack([np.tile(inv, P // half), sign], axis=1).astype(np.float32),
            "pool_const": np.stack([w / np.minimum(t, w) for w in WINDOWS]).astype(np.float32)}


def kernel(**inputs):
    import numpy as _np
    import concourse.bacc as _bacc
    from concourse import mybir as _mybir
    from concourse.bass_utils import run_bass_kernel_spmd as _run

    nc = _bacc.Bacc("TRN2", target_bir_lowering=False, num_devices=1)
    arrays = {name: _np.ascontiguousarray(inputs[name]) for name in _INS}
    arrays.update(shape_constants())
    aps = {name: nc.dram_tensor(name, a.shape, _mybir.dt.from_np(a.dtype), kind="ExternalInput").ap()
           for name, a in arrays.items()}
    out = nc.dram_tensor("out", (1, S, D), _mybir.dt.float32, kind="ExternalOutput").ap()
    build_program(nc, named(aps), out[0])
    r = _run(nc, [arrays], core_ids=[0])
    return r.results[0]["out"]
```

```python
from contextlib import ExitStack

import numpy as np

import concourse.bass as bass
from concourse import mybir
from concourse.alu_op_type import AluOpType as ALU

ACT = mybir.ActivationFunctionType
F32 = mybir.dt.float32
F32R = mybir.dt.float32r
I32 = mybir.dt.int32
U32 = mybir.dt.uint32
AX_X = mybir.AxisListType.X

P = 128
D = 1024
S = 512
KT = D // P
TT = S // P
CW = 256
NEG = -1e30
EPS = 1e-6

GH, GDK, GDV, GC = 4, 128, 256, 64
GN = S // GC
G_Q, G_K, G_V, G_R, G_Z = 0, 512, 1024, 2048, 2064
GNORM = 16.0
CAP = 44.0

NG, NHG, NDH = 4, 4, 64
NC, NCP = 31, 32
CB, CS = 32, 16
KV_PAD = 528
N_Q, N_KC, N_VC, N_KS, N_VS, N_KW, N_VW, N_GL, N_Z = 0, 1024, 1280, 1536, 1792, 2048, 2304, 2560, 2608
ROUND = 1.5 * 2.0 ** 23
TWO_PI = (6.28125, 0.0019350051879882812, 3.0199159819567e-07)
PI_DOWN = 3.1415925

HH = 16
H_Q, H_K, H_V, H_ZA, H_U, H_ZB, H_MA, H_MB = range(0, 8 * D, D)
WINDOWS = (2, 4, 8, 16)

VECS = [("pre0", 8), ("pre1", 8), ("post0", 8), ("post1", 8), ("gain2", 8), ("final", 8), ("b_ada", 24),
        ("pool_scale", 8), ("c", 8), ("b_gk", 4), ("head_norm", 2)]
VAT = {}
_n = 0
for _name, _k in VECS:
    VAT[_name] = _n
    _n += _k
NVEC = _n


N_SMALL2 = 7
NPAIR = TT * 8
MOD_PAIR = 24


def build_program(nc, A, out):
    es = ExitStack()
    with es:
        mem = [nc.sbuf_base + 64 - nc.sbuf_base % 64]

        def sb(name, shape, dt=F32):
            n = 1
            for x in shape[1:]:
                n *= x
            n *= 4
            t = nc.alloc_sbuf_tensor_at(name, list(shape), dt, offset=mem[0])
            mem[0] += (n + 31) // 32 * 32
            assert mem[0] <= nc.sbuf_usable_end, (name, mem[0], nc.sbuf_usable_end)
            return t

        def sem(name):
            return es.enter_context(nc.semaphore(name))

        banks = es.enter_context(nc.psum_tensor("banks", [P, 8, S], F32))
        bank = [banks[:, i, :] for i in range(8)]

        xT = sb("xT", [P, KT, S])
        act_hi = sb("act_hi", [P, KT, S], F32R)
        act_lo = sb("act_lo", [P, KT, S], F32R)
        raw = sb("raw", [P, 2, KT, CW])
        w_hi = sb("w_hi", [P, 2, KT, CW], F32R)
        w_lo = sb("w_lo", [P, 2, KT, CW], F32R)
        ident = sb("ident", [P, P])
        ones = sb("ones", [P, P])
        vec = sb("vec", [P, NVEC])
        eps_col = sb("eps_col", [P, 1])
        mod = sb("mod", [P, 3 * KT])
        silu_c = sb("silu_c", [P, KT])
        tmp = sb("tmp", [P, 2, S])
        rstd = sb("rstd", [P, S])
        arena = mem[0]

        qk = sb("qk", [P, 2 * GH, S])
        gate_b = sb("gate_b", [P, GH, S])
        kd_t = sb("kd_t", [P, GH, S])
        v_tok = sb("v_tok", [P, TT, D])
        silu_z = sb("silu_z", [P, KT, S])
        att = sb("att", [P, GH, S])
        kd_tok = sb("kd_tok", [P, GH, TT, P])
        states = sb("states", [P, 2, GN, GDV])
        decay = sb("decay", [P, GH, GN])
        neg_bgk = sb("neg_bgk", [P, GH])
        causal = sb("causal", [P, P], U32)
        chunk_keep = sb("chunk_keep", [P, S])
        glr_t = sb("glr_t", [16, S])
        w_up = sb("w_up", [16, S])
        head_sel = sb("head_sel", [P, 2 * GH - 1])


        def over(name, shape, base, dt=F32, at=None):
            return nc.alloc_sbuf_tensor_at(name, shape, dt, offset=base.manual_sbuf_range[0] if at is None else at)

        x_tok = over("x_tok", [P, TT, D], v_tok)
        vec_rows = over("vec_rows", [P, P], silu_z)
        y_t = over("y_t", [P, KT, S], qk)
        y_sq = over("y_sq", [P, KT, S], silu_z)
        o_t = over("o_t", [P, KT, S], gate_b)
        exps = over("exps", [P, 2, 3, S], states)
        head_std = over("head_std", [P, S], kd_tok)

        mem[0] = arena
        qT = sb("qT", [P, 8, S])
        silu_z2 = sb("silu_z2", [P, KT, S])
        kv_full = sb("kv_full", [P, NG, KV_PAD])
        rope_a = sb("rope_a", [P, 2, S])
        rope_b = sb("rope_b", [P, 2, S])
        kv_hi = sb("kv_hi", [P, NG + 1, KV_PAD], F32R)
        kv_lo = sb("kv_lo", [P, NG + 1, KV_PAD], F32R)
        ksT = sb("ksT", [P, 2, S])
        kwT = sb("kwT", [P, 2, S])
        v_tok2 = sb("v_tok2", [P, TT, 2, CW])
        cosT, sinT = sb("cosT", [P, S]), sb("sinT", [P, S])
        perm = sb("perm", [P, P])
        identb, maskb = sb("identb", [P, P], mybir.dt.bfloat16), sb("maskb", [P, P], mybir.dt.bfloat16)
        gates = sb("gates", [P, TT, 48])
        gate_bias = sb("gate_bias", [48, 1])
        gates_t = sb("gates_t", [48, S])
        rope_c = sb("rope_c", [P, 2])
        pe_t = sb("pe_t", [P, 2, CB // 2])
        hid_bias = sb("hid_bias", [P, 2])
        hid = sb("hid", [P, 2, NG * NCP])
        w2k, w2v = sb("w2k", [P, 2, NDH]), sb("w2v", [P, 2, NDH])
        kcmpT = sb("kcmpT", [P, NG * NCP])
        vcmp = sb("vcmp", [P, NG, CW])
        cmask = sb("cmask", [P, TT, NCP])
        cvalid = sb("cvalid", [P, TT, NCP])
        pcT = sb("pcT", [P, NG, P])
        cstat = sb("cstat", [P, 3, 16])
        wstat = sb("wstat", [P, 4, 2, 4])
        oT = over("oT", [P, KT, S], kv_full)
        prob = over("prob", [P, 3, 2, S], kv_hi)
        probT = over("probT", [P, 2, 2, 2, S], act_lo)
        y_t2 = over("y_t2", [P, KT, S], qT)
        y_sq2 = over("y_sq2", [P, KT, S], silu_z2)
        rope_q = over("rope_q", [P, 2, 2, S], silu_z2)

        def rope_at(r):
            return (rope_q[:, 0], rope_q[:, 1]) if r // 2 % 2 else (rope_a[:], rope_b[:])

        csc = tmp[:]
        hid4 = tmp[:]
        ada_sum = over("ada_sum", [P, 12, CW], w_lo)
        wide_zero = pcT[:, 0, :]
        pe_rows = pcT[0:CB, 1, :]

        mem[0] = arena
        br_hi, br_lo = sb("br_hi", [P, KT, S], F32R), sb("br_lo", [P, KT, S], F32R)
        qh, kh = sb("qh", [P, 2, 2, S]), sb("kh", [P, 2, 2, S])
        vh, zh = sb("vh", [P, 2, TT, CW]), sb("zh", [P, 2, 2, S])
        mix_a = sb("mix_a", [P, KT, S])
        ln_z = sb("ln_z", [P, 10, P])
        sp_hi = sb("sp_hi", [P, 10, P], F32R)
        w_z = sb("w_z", [P, 10, P])
        gated = sb("gated", [P, 2, S])
        tri = sb("tri", [P, P])
        minus = sb("minus", [P, P])
        tri_r, minus_r = sb("tri_r", [P, P], F32R), sb("minus_r", [P, P], F32R)
        identb3, maskb3 = sb("identb3", [P, P], mybir.dt.bfloat16), sb("maskb3", [P, P], mybir.dt.bfloat16)
        pool_fix = sb("pool_fix", [P, 4, 16])
        gain_mod = sb("gain_mod", [P, KT])
        sp_lo = over("sp_lo", [P, 10, P], w_z, F32R)
        pool_u = over("pool_u", [P, KT, S], qh)
        silu_zb = over("silu_zb", [P, KT, S], vh)
        mix_b = over("mix_b", [P, KT, S], ln_z)
        sums = [over("sums0", [P, 2, S], ln_z), over("sums1", [P, 2, S], sp_hi)]
        x_sq = over("x_sq", [P, KT, S], ln_z)
        out_tok = over("out_tok", [P, TT, D], qh)

        consts_ready = sem("consts_ready")
        x_landed = [sem(f"x_landed{i}") for i in range(2)]
        vec_landed, up_landed = sem("vec_landed"), sem("up_landed")
        raw_landed = [sem(f"raw_landed{i}") for i in range(2)]
        hi_done, lo_done = sem("hi_done"), sem("lo_done")
        bank_full = [sem(f"bank_full{i}") for i in range(4)]
        bank_free = [sem(f"bank_free{i}") for i in range(4)]
        xt_full, xt_copied, vec_full, vec_ready = sem("xt_full"), sem("xt_copied"), sem("vec_full"), sem("vec_ready")
        sq_ready, squares_summed, sq_used, rstd_ready = sem("sq_ready"), sem("squares_summed"), sem("sq_used"), sem("rstd_ready")
        scaled, act_hi_done, h_ready = sem("scaled"), sem("act_hi_done"), sem("h_ready")
        y_scaled, x_even, x_odd = sem("y_scaled"), sem("x_even"), sem("x_odd")
        dve_chain = sem("dve_chain")
        act_chain = sem("act_chain")
        pool_chain = sem("pool_chain")
        up_full, nu_ready, ln_ready = sem("up_full"), sem("nu_ready"), sem("ln_ready")
        gsum_ready, grow_ready, exps_ready, exps_used = sem("gsum_ready"), sem("grow_ready"), sem("exps_ready"), sem("exps_used")
        kd_ready, kdt_full, kdtok_ready = sem("kd_ready"), sem("kdt_full"), sem("kdtok_ready")
        att_full, att_ready = sem("att_full"), sem("att_ready")
        upd_full, upd_read, state_ready = sem("upd_full"), sem("upd_read"), sem("state_ready")
        o_full, o_squared, o_read = sem("o_full"), sem("o_squared"), sem("o_read")
        osq_used, orstd_ready, obc_full = sem("osq_used"), sem("orstd_ready"), sem("obc_full")
        out_full, out_left, out_right, stored = sem("out_full"), sem("out_left"), sem("out_right"), sem("stored")

        small2_landed, consts2_ready = sem("small2_landed"), sem("consts2_ready")
        pe_full, pe_ready = sem("pe_full"), sem("pe_ready")
        angle_ready, table_ready = sem("angle_ready"), sem("table_ready")
        turn_ready, turn_full, turned = sem("turn_ready"), sem("turn_full"), sem("turned")
        kv_ready, kv_hi_done, kv_split = sem("kv_ready"), sem("kv_hi_done"), sem("kv_split")
        hid_bias_ready, hid_ready = sem("hid_bias_ready"), sem("hid_ready")
        cmp_full, cmp_ready = sem("cmp_full"), sem("cmp_ready")
        gates_t_ready, gates_full, gate_ready = sem("gates_t_ready"), sem("gates_full"), sem("gate_ready")
        c_scores, c_shifted, c_exp, c_prob = sem("c_scores"), sem("c_shifted"), sem("c_exp"), sem("c_prob")
        c_tfull, c_tcopied, c_out, c_taken = sem("c_tfull"), sem("c_tcopied"), sem("c_out"), sem("c_taken")
        s_full, s_max, s_exp, p_ready = sem("s_full"), sem("s_max"), sem("s_exp"), sem("p_ready")
        t_full, t_sel, t_win = sem("t_full"), sem("t_sel"), sem("t_win")
        pv_full, pv_read, o_gated = sem("pv_full"), sem("pv_read"), sem("o_gated")
        ot_high, ot_low = sem("ot_high"), sem("ot_low")

        silu_c_ready, ada_summed, mod_full, mod_ready = sem("silu_c_ready"), sem("ada_summed"), sem("mod_full"), sem("mod_ready")
        consts3_ready, small3_landed = sem("consts3_ready"), sem("small3_landed")
        z_full, zc_ready, e_ready, l_ready, sp_ready = sem("z_full"), sem("zc_ready"), sem("e_ready"), sem("l_ready"), sem("sp_ready")
        tri_full, w_ready, hv_full, head_gated = sem("tri_full"), sem("w_ready"), sem("hv_full"), sem("head_gated")
        pair_high, pair_low = sem("pair_high"), sem("pair_low")
        d_ready, d_high, d_low, mix_full, mix_taken = sem("d_ready"), sem("d_high"), sem("d_low"), sem("mix_full"), sem("mix_taken")
        x_final, fin_ready = sem("x_final"), sem("fin_ready")

        def cols(m, at, n=CW):
            return m[:, bass.ds(at, n)].rearrange("(k p) n -> p k n", p=P)

        C_GLR, C_Q, C_K, C_V, C_Z, C_GOUT = 0, 1, 3, 5, 9, 13
        C_KC, C_KS, C_VC, C_KW, C_CK, C_VS, C_VW, C_CV, C_GL, C_NQ, C_NZ, C_ADA, C_NOUT = (
            17, 18, 19, 20, 21, 23, 24, 25, 27, 28, 32, 36, 48)
        C_H, C_MA, C_U, C_BA, C_ZB, C_MB, C_MIX, C_BB, C_OUT = 52, 68, 72, 76, 80, 84, 88, 89, 93
        C_END = 97
        w3 = A["w_in_2"]
        w2, wo2, ck, cv = A["nsa_w_in"], A["nsa_w_out"], A["nsa_ck_w1"], A["nsa_cv_w1"]
        w1, wo1 = A["gla_w_in"], A["gla_w_out"]
        groups = [(C_GLR, 1, w1, G_R), (C_Q, 2, w1, G_Q), (C_K, 2, w1, G_K), (C_V, 4, w1, G_V),
                  (C_Z, 4, w1, G_Z), (C_GOUT, 4, wo1, 0)]
        groups2 = [(C_KC, 1, w2, N_KC), (C_KS, 1, w2, N_KS), "small", (C_VC, 1, w2, N_VC), (C_KW, 1, w2, N_KW),
                   (C_CK, 2, ck, None), (C_VS, 1, w2, N_VS), (C_VW, 1, w2, N_VW), (C_CV, 2, cv, None),
                   (C_GL, 1, w2, N_GL), (C_NQ, 4, w2, "q"), (C_NZ, 4, w2, "z"), (C_ADA, 12, A["w_ada_2"], 0), (C_NOUT, 4, wo2, "rows")]
        groups3 = [(C_MA, 4, w3, H_MA), "small", (C_U, 4, w3, H_U), (C_BA, 4, A["w_branch_a_2"], 0),
                   (C_ZB, 4, w3, H_ZB), (C_MB, 4, w3, H_MB), (C_MIX, 1, A["pool_w_2"], 0),
                   (C_BB, 4, A["w_branch_b_2"], 0), (C_OUT, 4, A["w_out_2"], 0)]

        def vcol(name, j):
            return vec[:, VAT[name] + j:VAT[name] + j + 1]

        def blocks(x, st):
            at = (0, 4, 7, 9)[st]
            return x[:, at:at + TT - st].rearrange("p b q -> p (b q)")

        def banks_free(eng, c):
            for b in range(4):
                eng.wait_ge(bank_free[b], (c + 1 - b // 2) // 2)

        def x_is_updated(eng, layer):
            eng.wait_ge(x_even, KT // 2 * layer)
            eng.wait_ge(x_odd, KT // 2 * layer)

        def update_at(n):
            return bank[4 + 2 * (n % 2) + n // 4][:, n // 2 % 2 * GDV:(n // 2 % 2 + 1) * GDV]

        block = es.enter_context(nc.Block())

        @block.sync
        def _(sp):
            for half in range(2):
                sp.dma_start(x_tok[:, :, half * S:(half + 1) * S],
                             A["x"].rearrange("(t p) d -> p t d", p=P)[:, :, half * S:(half + 1) * S])\
                    .then_inc(x_landed[half], 16)
            for name, n in VECS:
                sp.dma_start(vec_rows[VAT[name]:VAT[name] + n, :],
                             A[name].rearrange("(k p) -> k p", p=P)).then_inc(vec_landed, 16)
            sp.dma_start(w_up[:], A["gla_w_gk_up"]).then_inc(up_landed, 16)

            def load(c, u, m, at):
                if not (isinstance(c, int) and c < 2):
                    sp.wait_ge(lo_done, c - 1)
                sp.dma_start(raw[:, u], cols(m, at)).then_inc(raw_landed[u], 16)

            for c0, n, m, at in groups:
                if n < 4 or c0 < 2:
                    for j in range(n):
                        load(c0 + j, (c0 + j) % 2, m, at + j * CW)
                else:
                    with sp.Fori(0, n // 2) as i:
                        for u in range(2):
                            load(2 * i + (c0 + u), (c0 + u) % 2, m, 2 * CW * i + (at + u * CW))
            for group in groups2:
                if group == "small":
                    x_is_updated(sp, 1)
                    pos = A["positions"].rearrange("(o s) -> o s", o=1).broadcast_to([P, S])
                    small = [(rope_a[:, 0].bitcast(I32), pos), (rope_c[:], A["rope_const"]),
                             (gate_bias[:], A["nsa_b_gate"].rearrange("(s o) -> s o", o=1))]
                    small += [(w[:], A[n].rearrange("(k p) d -> p k d", p=P)) for w, n in ((w2k, "nsa_ck_w2"), (w2v, "nsa_cv_w2"))]
                    small += [(pe_rows[CB // 2 * i:CB // 2 * (i + 1), :], A[n].rearrange("(m h) d -> m (h d)", h=2))
                              for i, n in enumerate(("nsa_pe_k", "nsa_pe_v"))]
                    assert len(small) == N_SMALL2
                    for dst, src in small:
                        sp.dma_start(dst, src).then_inc(small2_landed, 16)
                    continue
                c0, n, m, at = group
                if at in ("q", "z"):
                    first_col = N_Q if at == "q" else N_Z
                    for j in range(4):
                        u = (c0 + j) % 2
                        sp.wait_ge(lo_done, c0 + j - 1)
                        for h in range(2):
                            for g in range(2):
                                sp.dma_start(raw[:, u, :, h * P + g * NDH:h * P + (g + 1) * NDH],
                                             cols(m, first_col + j // 2 * 512 + g * CW + (j % 2 * 2 + h) * NDH, NDH))\
                                    .then_inc(raw_landed[u], 16)
                elif at == "rows":
                    for j in range(4):
                        u = (c0 + j) % 2
                        sp.wait_ge(lo_done, c0 + j - 1)
                        rows = m[:, j * CW:(j + 1) * CW].rearrange("(a h j d) n -> a h d j n", a=2, h=2, j=4)
                        for a in range(2):
                            for h in range(2):
                                sp.dma_start(raw[h * NDH:(h + 1) * NDH, u, 4 * a:4 * a + 4, :], rows[a, h])\
                                    .then_inc(raw_landed[u], 16)
                elif at is None:
                    for j in range(2):
                        sp.wait_ge(lo_done, c0 + j - 1)
                        sp.dma_start(raw[:, (c0 + j) % 2], m[j * D:(j + 1) * D, :].rearrange("(k p) n -> p k n", p=P))\
                            .then_inc(raw_landed[(c0 + j) % 2], 16)
                elif n < 4:
                    load(c0, c0 % 2, m, at)
                else:
                    with sp.Fori(0, n // 2) as i:
                        for u in range(2):
                            load(2 * i + (c0 + u), (c0 + u) % 2, m, 2 * CW * i + (at + u * CW))
            for kind, at in enumerate((H_Q, H_K, H_V, H_ZA)):
                load(C_H + kind, (C_H + kind) % 2, w3, at)
            with sp.Fori(0, 3) as i:
                for kind, at in enumerate((H_Q, H_K, H_V, H_ZA)):
                    load(4 * i + (C_H + 4 + kind), (C_H + kind) % 2, w3, CW * i + (at + CW))
            for group in groups3:
                if group == "small":
                    x_is_updated(sp, 2)
                    fix = A["pool_const"].rearrange("(o g) t -> o g t", o=1).broadcast_to([P, 4, 16])
                    sp.dma_start(pool_fix[:], fix).then_inc(small3_landed, 16)
                    continue
                c0, n, m, at = group
                if n < 4:
                    load(c0, c0 % 2, m, at)
                else:
                    with sp.Fori(0, n // 2) as i:
                        for u in range(2):
                            load(2 * i + (c0 + u), (c0 + u) % 2, m, 2 * CW * i + (at + u * CW))
            for t in range(TT):
                sp.wait_ge(out_left, t + 1)
                sp.dma_start(out[t * P:(t + 1) * P, 0:S], out_tok[:, t, 0:S]).then_inc(stored, 16)
            for t in range(TT):
                if t % 2:
                    sp.wait_ge(out_left, TT + (t + 1) // 2)
                else:
                    sp.wait_ge(out_right, t // 2 + 1)
                sp.dma_start(out[t * P:(t + 1) * P, S:D], out_tok[:, t, S:D]).then_inc(stored, 16)
            sp.wait_ge(stored, 2 * 16 * TT)

        @block.gpsimd
        def _(pool):
            chained = [0]

            def link(ins):
                chained[0] += 1
                ins.then_inc(pool_chain, 1)
                pool.wait_ge(pool_chain, chained[0])

            pool.memset(ones[:], 1.0)
            pool.memset(eps_col[:], EPS)
            pool.memset(head_sel[:], 0.0)
            pool.memset(att[:], 0.0)
            pool.memset(chunk_keep[:], 1.0)
            link(pool.memset(ident[:], 0.0))
            pool.memset(head_sel[:, GH - 1:GH], 1.0)
            pool.memset(chunk_keep[:].rearrange("p (n c) -> p n c", c=GC)[:, :, 0:1], 0.0)
            link(pool.affine_select(out=ident[:], in_=ident[:], compare_op=ALU.not_equal, fill=1.0, base=0,
                                    pattern=[[-1, P]], channel_multiplier=1))
            link(pool.affine_select(out=tmp[:, 0, 0:P], in_=ones[:], compare_op=ALU.is_ge, fill=0.0, base=0,
                                    pattern=[[1, P]], channel_multiplier=-1))
            link(pool.memset(tmp[0:GC, 0, GC:P], 0.0))
            link(pool.tensor_copy(causal[:], tmp[:, 0, 0:P]))
            pool.memset(rstd[:, 0:1], 0.0).then_inc(consts_ready, 1)

            def split_low(c, u):
                pool.wait_ge(hi_done, c + 1)
                pool.tensor_tensor(w_lo[:, u], raw[:, u], w_hi[:, u].bitcast(F32), ALU.subtract).then_inc(lo_done, 1)

            def split_range(c0, c1):
                pairs = (c1 - c0) // 2
                if pairs > 1:
                    with pool.Fori(0, pairs) as i:
                        for u in range(2):
                            split_low(2 * i + (c0 + u), (c0 + u) % 2)
                    c0 += 2 * pairs
                for c in range(c0, c1):
                    split_low(c, c % 2)

            def add_odd(layer, y):
                for k in range(1, KT, 2):
                    pool.wait_ge(y_scaled, KT * (layer - 1) + k + 1)
                    pool.tensor_tensor(xT[:, k], xT[:, k], y[:, k], ALU.add).then_inc(x_odd, 1)

            split_range(0, C_KC + 1)
            add_odd(1, y_t)
            x_is_updated(pool, 1)
            pool.memset(kv_full[:], 0.0)
            pool.memset(vcmp[:], 0.0)
            link(pool.memset(cvalid[:], 1.0))
            link(pool.affine_select(out=cvalid[:], in_=cvalid[:], compare_op=ALU.is_ge, fill=0.0, base=1 - CB,
                                    pattern=[[P, TT], [-CS, NCP]], channel_multiplier=1))
            pool.tensor_scalar(cmask[:], cvalid[:], -1.0, -NEG, ALU.add, ALU.mult)
            for t in range(2):
                two = lambda a: a.rearrange("p (a two w) -> p a two w", two=2, w=32)
                pool.tensor_copy(two(perm[:])[:, :, t], two(ident[:])[:, :, 1 - t])
            pool.tensor_copy(identb[:], ident[:])
            link(pool.memset(wide_zero, 0.0))
            link(pool.affine_select(out=wide_zero, in_=wide_zero, compare_op=ALU.is_ge, fill=NEG, base=0,
                                    pattern=[[-1, P]], channel_multiplier=1))
            pool.tensor_copy(maskb[:], wide_zero)
            pool.memset(kv_hi[:, NG].bitcast(F32), 0.0)
            link(pool.memset(kv_lo[:, NG].bitcast(F32), 0.0))
            pool.sem_inc(consts2_ready, 1)
            split_range(C_KC + 1, C_ADA)
            pool.wait_ge(silu_c_ready, 1)
            for u in range(2):
                pool.wait_ge(bank_full[2 * u + 1], C_ADA // 2)
            for i in range(C_NOUT - C_ADA):
                c = C_ADA + i
                u = c % 2
                pool.wait_ge(raw_landed[u], 16 * (c // 2) + 16 + 4 * 48)
                scale = silu_c[:].rearrange("p (k o) -> p k o", o=1).broadcast_to([P, KT, CW])
                link(pool.tensor_tensor(raw[:, u], raw[:, u], scale, ALU.mult))
                link(pool.tensor_tensor(raw[:, u, 0:4], raw[:, u, 0:4], raw[:, u, 4:8], ALU.add))
                link(pool.tensor_tensor(raw[:, u, 0:2], raw[:, u, 0:2], raw[:, u, 2:4], ALU.add))
                link(pool.tensor_tensor(ada_sum[:, i], raw[:, u, 0], raw[:, u, 1], ALU.add))
                pool.sem_inc(lo_done, 1)
            pool.sem_inc(ada_summed, 1)
            split_range(C_NOUT, C_H + 1)
            add_odd(2, y_t2)
            x_is_updated(pool, 2)
            link(pool.memset(minus[:], -1.0))
            link(pool.affine_select(out=tri[:], in_=minus[:], compare_op=ALU.is_ge, fill=0.0, base=0,
                                    pattern=[[-1, P]], channel_multiplier=1))
            pool.tensor_copy(identb3[:], ident[:])
            pool.tensor_copy(tri_r[:], tri[:])
            pool.tensor_copy(minus_r[:], minus[:])
            link(pool.memset(w_z[:, 0], 0.0))
            link(pool.affine_select(out=w_z[:, 0], in_=w_z[:, 0], compare_op=ALU.is_gt, fill=NEG, base=0,
                                    pattern=[[1, P]], channel_multiplier=-1))
            pool.tensor_copy(maskb3[:], w_z[:, 0]).then_inc(consts3_ready, 1)
            split_range(C_H + 1, C_END)

        @block.scalar
        def _(act):
            chained = [0]

            def link(ins):
                chained[0] += 1
                ins.then_inc(act_chain, 1)
                act.wait_ge(act_chain, chained[0])

            more = [0, 0]

            def split_high(c, half, u, first=False):
                if isinstance(c, int) and (C_NQ <= c < C_ADA or C_NOUT <= c < C_NOUT + 4):
                    more[u] += 48
                act.wait_ge(raw_landed[u], 16 * half + 16 + more[u])
                if not first:
                    act.wait_ge(bank_full[2 * u + 1], half)
                act.activation(w_hi[:, u], raw[:, u], ACT.Copy).then_inc(hi_done, 1)

            def stream(c0, n, take):
                def step(c, half, nhalf, u, j):
                    split_high(c + 1, nhalf, 1 - u)
                    for m in range(2):
                        act.wait_ge(bank_full[2 * u + m], half + 1)
                        take(j, m, bank[2 * u + m]).then_inc(bank_free[2 * u + m], 1)
                if n < 4:
                    for j in range(n):
                        c = c0 + j
                        step(c, c // 2, (c + 1) // 2, c % 2, j)
                else:
                    with act.Fori(0, n // 2) as i:
                        for v in range(2):
                            c = c0 + v
                            step(2 * i + c, i + c // 2, i + (c + 1) // 2, c % 2, 2 * i + v)

            def ln_and_exp():
                act.preload_act_table_set("natural_log_exp_and_others")

            def norm_front(n):
                ln_and_exp()
                for k in range(KT):
                    if n == 0:
                        act.wait_ge(xt_copied, k + 1)
                    else:
                        act.wait_ge(x_odd if k % 2 else x_even, KT // 2 * (n // 2 - 1) + k // 2 + 1)
                    if k >= 2:
                        act.wait_ge(sq_used, KT * n + k - 1)
                    act.activation(tmp[:, k % 2], xT[:, k], ACT.Square).then_inc(sq_ready, 1)

            def root(n):
                act.wait_ge(sq_used, KT * (n + 1))
                link(act.activation(rstd[:], bank[4][:], ACT.Ln, scale=1.0 / D, bias=eps_col[:]))
                act.activation(rstd[:], rstd[:], ACT.Exp, scale=-0.5).then_inc(rstd_ready, 1)

            def high_parts(n, hi=act_hi, tiles=range(KT), shift=None, split=None):
                for k in tiles:
                    if split is not None and k == 2:
                        split_high(split, split // 2, split % 2, first=(split < 2))
                    act.wait_ge(scaled, KT * n + k + 1)
                    if shift is None:
                        part = act.activation(hi[:, k], tmp[:, k % 2], ACT.Copy)
                    else:
                        part = act.activation(hi[:, k], tmp[:, k % 2], ACT.Identity, bias=shift[:, k:k + 1])
                    part.then_inc(act_hi_done, 1)

            def step2(c, take, ahead=True):
                if ahead:
                    split_high(c + 1, (c + 1) // 2, (c + 1) % 2)
                u = c % 2
                for m in range(2):
                    act.wait_ge(bank_full[2 * u + m], c // 2 + 1)
                    take(m, bank[2 * u + m]).then_inc(bank_free[2 * u + m], 1)

            def stream_out(c0, n, y, y_sq):
                ln_and_exp()
                for j in range(4):
                    def take(m, b):
                        act.activation(y[:, 2 * j + m, :], b, ACT.Copy)
                        return act.activation(y_sq[:, 2 * j + m, :], b, ACT.Square)
                    step2(c0 + j, take, ahead=(j > 0))
                root(n)

            act.wait_ge(consts_ready, 1)
            norm_front(0)
            split_high(0, 0, 0, first=True)
            root(0)
            split_high(1, 0, 1, first=True)
            high_parts(0)

            act.wait_ge(bank_full[1], 1)
            act.activation(glr_t[:], bank[1][0:16, :], ACT.Copy).then_inc(bank_free[1], 1)
            act.sem_inc(bank_free[0], 1)
            stream(C_Q, 2, lambda j, m, b: act.activation(qk[:, 2 * j + m], b[:], ACT.Copy, scale=GDK ** -0.5))
            split_high(C_K + 1, (C_K + 1) // 2, (C_K + 1) % 2)
            ln_and_exp()
            for h in range(GH):
                act.wait_ge(nu_ready, h + 1)
                link(act.activation(kd_t[:, h], kd_t[:, h], ACT.Exp))
                act.activation(kd_t[:, h], kd_t[:, h], ACT.Ln, bias=1.0).then_inc(ln_ready, 1)
            for j in range(2):
                step2(C_K + j, lambda m, b: act.activation(qk[:, GH + 2 * j + m], b, ACT.Copy), ahead=(j > 0))

            def chunk_exps(h):
                act.wait_ge(gsum_ready, h + 1)
                if h >= 2:
                    act.wait_ge(exps_used, h - 1)
                act.activation(exps[:, h % 2, 0], gate_b[:, h], ACT.Exp, scale=-1.0 / GNORM)
                act.activation(exps[:, h % 2, 1], gate_b[:, h], ACT.Exp, scale=1.0 / GNORM)
                act.wait_ge(grow_ready, h + 1)
                act.activation(exps[:, h % 2, 2], kd_t[:, h], ACT.Exp, scale=1.0 / GNORM).then_inc(exps_ready, 1)
            for j in range(4):
                step2(C_V + j, lambda m, b: act.activation(
                    v_tok[:, 2 * m:2 * m + 2, j * CW:(j + 1) * CW], b.rearrange("p (t n) -> p t n", t=2), ACT.Copy))
                chunk_exps(j)
            for j in range(4):
                step2(C_Z + j, lambda m, b: act.activation(silu_z[:, 2 * j + m, :], b, ACT.Silu))
                if j == 1:
                    for h in range(GH):
                        act.wait_ge(kdt_full, h + 1)
                        act.activation(kd_tok[:, h], bank[4 + h][:], ACT.Copy).then_inc(kdtok_ready, 1)
            ln_and_exp()
            for t in range(2 * GH):
                act.wait_ge(o_full, t + 1)
                if t >= 2:
                    act.wait_ge(osq_used, t - 1)
                act.activation(tmp[:, t % 2], bank[t % 3][:], ACT.Square).then_inc(o_squared, 1)
            act.wait_ge(osq_used, 2 * GH)
            link(act.activation(head_std[0:GH, :], bank[3][0:GH, :], ACT.Ln, scale=1.0 / GDV, bias=eps_col[0:GH, :]))
            act.activation(head_std[0:GH, :], head_std[0:GH, :], ACT.Exp, scale=-0.5).then_inc(orstd_ready, 1)
            high_parts(1, split=C_GOUT + 1)
            stream_out(C_GOUT, 1, y_t, y_sq)

            norm_front(2)
            root(2)
            high_parts(2, split=C_KS)

            def untaken(c, n=1):
                for c in range(c, c + n):
                    split_high(c + 1, (c + 1) // 2, (c + 1) % 2)

            def unused_banks(c):
                act.sem_inc(bank_free[c % 2 * 2], 1)
                act.sem_inc(bank_free[c % 2 * 2 + 1], 1)

            def kv_high(i):
                act.wait_ge(kv_ready, i + 1)
                act.wait_ge(pe_ready, 1)
                act.wait_ge(consts2_ready, 1)
                act.activation(kv_hi[:, 0:NG], kv_full[:], ACT.Copy)
                act.activation(kv_hi[:, NG, 0:CB:2], pe_t[:, i], ACT.Copy).then_inc(kv_hi_done, 1)

            def hidden(i):
                act.wait_ge(hid_bias_ready, i + 1)
                for m in range(2):
                    src = bank[6 + m][:, 0:NG * NCP]
                    if i == 0:
                        act.activation(hid[:, m], src, ACT.Silu, bias=hid_bias[:, m:m + 1]).then_inc(hid_ready, 1)
                    else:
                        act.activation(hid4[:, m].rearrange("p (g h c) -> p g h c", g=NG, h=NHG),
                                       src.rearrange("p (g o c) -> p g o c", g=NG, o=1).broadcast_to([P, NG, NHG, NCP]),
                                       ACT.Silu, bias=hid_bias[:, m:m + 1]).then_inc(hid_ready, 1)

            untaken(C_KS)
            act.wait_ge(angle_ready, 2)
            act.activation(sinT[:], sinT[:], ACT.Sin, scale=rope_c[:, 1:2]).then_inc(table_ready, 1)
            act.activation(cosT[:], cosT[:], ACT.Sin).then_inc(table_ready, 1)
            split_high(C_VC + 1, (C_VC + 1) // 2, (C_VC + 1) % 2)
            kv_high(0)
            for m in range(2):
                u = C_VC % 2
                act.wait_ge(bank_full[2 * u + m], C_VC // 2 + 1)
                if m == 0:
                    act.wait_ge(kv_split, 1)
                for g in range(2):
                    half = bank[2 * u + m][g * NDH:(g + 1) * NDH, :]
                    act.activation(kv_full[0:NDH, 2 * m + g, 0:S], half, ACT.Copy)
                    last = act.activation(kv_full[NDH:P, 2 * m + g, 0:S - 1], half[:, 1:S], ACT.Copy)
                last.then_inc(bank_free[2 * u + m], 1)
            act.wait_ge(bank_free[2 * (C_VC % 2)], C_VC // 2 + 1)
            act.wait_ge(bank_free[2 * (C_VC % 2) + 1], C_VC // 2 + 1)
            act.sem_inc(kv_ready, 1)
            untaken(C_KW)
            for c in (C_CK, C_CK + 1):
                unused_banks(c)
                untaken(c)
            act.wait_ge(bank_full[2 * ((C_CK + 1) % 2) + 1], (C_CK + 1) // 2 + 1)
            kv_high(1)
            hidden(0)
            for c in (C_VS, C_VW):
                step2(c, lambda m, b, w=c - C_VS: act.activation(
                    v_tok2[:, 2 * m:2 * m + 2, w, :], b.rearrange("p (t n) -> p t n", t=2), ACT.Copy))
            for c in (C_CV, C_CV + 1):
                unused_banks(c)
                untaken(c)
            hidden(1)
            untaken(C_GL)
            u = C_GL % 2
            act.wait_ge(bank_full[2 * u + 1], C_GL // 2 + 1)
            act.activation(gates_t[:], bank[2 * u + 1][0:48, :], ACT.Sigmoid, bias=gate_bias[:]).then_inc(bank_free[2 * u + 1], 1)
            act.sem_inc(bank_free[2 * u], 1)
            act.wait_ge(bank_free[2 * u + 1], C_GL // 2 + 1)
            act.sem_inc(gates_t_ready, 1)
            untaken(C_NQ, 4)
            for t in range(TT):
                c = C_NZ + t
                if t < 3:
                    split_high(c + 1, (c + 1) // 2, (c + 1) % 2)
                act.wait_ge(c_shifted, t + 1)
                act.activation(csc[:, 1], csc[:, 0], ACT.Exp, scale=NDH ** -0.5).then_inc(c_exp, 1)
                act.wait_ge(c_tfull, t + 1)
                if t:
                    act.wait_ge(c_out, t)
                act.activation(pcT[:].rearrange("p g q -> p (g q)"), bank[6][:], ACT.Copy).then_inc(c_tcopied, 1)
                for m in range(2):
                    b = 2 * (c % 2) + m
                    act.wait_ge(bank_full[b], c // 2 + 1)
                    act.activation(silu_z2[:, 2 * t + m], bank[b], ACT.Silu).then_inc(bank_free[b], 1)
            act.sem_inc(hi_done, 1)

            act.activation(silu_c[:], vec[:, VAT["c"]:VAT["c"] + KT], ACT.Silu).then_inc(silu_c_ready, 1)
            act.sem_inc(hi_done, C_NOUT - C_ADA - 1)

            def sel_turned(v):
                w = (v // 16 + 1) * P
                act.wait_ge(t_full, v + 1)
                if v >= 4:
                    act.wait_ge(pv_full, v // 2 - 1)
                act.activation(probT[:, v // 2 % 2, v % 2, 0, 0:w], bank[4][:, 0:w], ACT.Copy).then_inc(t_sel, 1)

            def exponentials(n):
                keys = (n // 16 + 1) * P
                act.wait_ge(s_max, n + 1)
                for w in range(2):
                    act.activation(prob[:, n % 3, w, 0:keys], bank[2 * (n % 2) + w][:, 0:keys], ACT.Exp,
                                   bias=wstat[:, n % 4, w, 1:2], scale=NDH ** -0.5,
                                   accum_out=wstat[:, n % 4, w, 2:3]).then_inc(s_exp, 1)

            for n in range(0, 2 * NPAIR + 2, 2):
                if n >= 4:
                    sel_turned(n - 3)
                if n >= 2:
                    sel_turned(n - 2)
                if n < 2 * NPAIR:
                    exponentials(n)
                    exponentials(n + 1)
                if n == 2 * MOD_PAIR + 4:
                    for b in range(4):
                        act.sem_inc(bank_free[b], (C_NOUT - C_ADA) // 2)
                    split_high(C_NOUT, C_NOUT // 2, C_NOUT % 2)
            sel_turned(2 * NPAIR - 1)
            split_high(C_NOUT + 1, (C_NOUT + 1) // 2, (C_NOUT + 1) % 2)
            act.wait_ge(o_gated, TT)
            for k in range(KT):
                act.activation(act_hi[:, k], oT[:, k], ACT.Copy).then_inc(ot_high, 1)
            stream_out(C_NOUT, 3, y_t2, y_sq2)

            norm_front(4)
            root(4)
            high_parts(3, shift=mod, split=C_H + 1)

            def taker(c):
                s, kind = (c - C_H) // 4 % 2, (c - C_H) % 4
                if c >= C_MA:
                    return lambda m, b: act.activation(mix_a[:, 2 * (c - C_MA) + m], b, ACT.Sigmoid)
                return (lambda m, b: act.activation(qh[:, s, m], b, ACT.Copy, scale=NDH ** -0.5),
                        lambda m, b: act.activation(kh[:, s, m], b, ACT.Copy),
                        lambda m, b: act.activation(vh[:, s, 2 * m:2 * m + 2], b.rearrange("p (t n) -> p t n", t=2), ACT.Copy),
                        lambda m, b: act.activation(zh[:, s, m], b, ACT.Silu))[kind]

            def take3(c, m):
                b = 2 * (c % 2) + m
                act.wait_ge(bank_full[b], c // 2 + 1)
                taker(c)(m, bank[b]).then_inc(bank_free[b], 1)

            def pair_split(p):
                act.wait_ge(head_gated, 2 * p + 2)
                act.activation(br_hi[:, p], gated[:, p % 2], ACT.Copy).then_inc(pair_high, 1)

            for c in range(C_H, C_H + 4):
                step2(c, taker(c), ahead=(c > C_H))
            for h in range(HH):
                c = C_H + 4 + h
                split_high(c + 1, (c + 1) // 2, (c + 1) % 2)
                for i, st in enumerate(range(TT - 1, -1, -1)):
                    act.wait_ge(zc_ready, TT * h + i + 1)
                    act.activation(blocks(ln_z, st), blocks(ln_z, st), ACT.Exp).then_inc(e_ready, 1)
                for i, st in enumerate(range(TT - 1, -1, -1)):
                    act.wait_ge(e_ready, TT * h + i + 1)
                    act.activation(blocks(ln_z, st), blocks(ln_z, st), ACT.Ln, bias=1.0).then_inc(l_ready, 1)
                take3(c, 0)
                if h % 2 == 0 and h:
                    pair_split(h // 2 - 1)
                act.wait_ge(tri_full, TT * (h + 1))
                for st in range(TT - 1, -1, -1):
                    act.activation(blocks(w_z, st), bank[4 + st][:, st * P:S], ACT.Exp).then_inc(w_ready, 1)
                take3(c, 1)
            pair_split(HH // 2 - 1)
            for c in range(C_U, C_U + 4):
                split_high(c + 1, (c + 1) // 2, (c + 1) % 2)
            for c in range(C_BA, C_BA + 4):
                split_high(c + 1, (c + 1) // 2, (c + 1) % 2)
            for j in range(4):
                step2(C_ZB + j, lambda m, b: act.activation(silu_zb[:, 2 * j + m, :], b, ACT.Silu))
                if j == 0:
                    for k in range(KT):
                        act.wait_ge(d_ready, k // 2 + 1)
                        act.activation(br_hi[:, k], pool_u[:, k], ACT.Copy).then_inc(d_high, 1)
            stream(C_MB, 4, lambda j, m, b: act.activation(mix_b[:, bass.ds(2 * j + m, 1), :], b, ACT.Sigmoid))
            unused_banks(C_MIX)
            split_high(C_MIX + 1, (C_MIX + 1) // 2, (C_MIX + 1) % 2)
            high_parts(4)
            for c in range(C_BB, C_BB + 4):
                split_high(c + 1, (c + 1) // 2, (c + 1) % 2)
                high_parts(5, br_hi, range(2 * (c - C_BB), 2 * (c - C_BB) + 2))
            ln_and_exp()
            for c in range(C_OUT, C_END):
                if c + 1 < C_END:
                    split_high(c + 1, (c + 1) // 2, (c + 1) % 2)
                for k in range(2 * (c - C_OUT), 2 * (c - C_OUT) + 2):
                    act.wait_ge(x_final, k + 1)
                    act.activation(x_sq[:, k], xT[:, k], ACT.Square).then_inc(sq_ready, 1)
            root(5)
            for t in range(TT):
                act.wait_ge(out_full, t + 1)
                act.activation(out_tok[:, t, 0:S], bank[t], ACT.Copy).then_inc(out_left, 1)
            for t in (1, 3):
                act.wait_ge(out_full, TT + t + 1)
                act.activation(out_tok[:, t, S:D], bank[4 + t], ACT.Copy).then_inc(out_left, 1)

        @block.tensor
        def _(pe):
            def arriving(c, ready, at, source=(act_hi, act_lo)):
                x_hi, x_lo = source
                u = c % 2
                pe.wait_ge(lo_done, c + 1)
                for m in range(2):
                    pe.wait_ge(bank_free[2 * u + m], c // 2)
                for k in range(KT):
                    pe.wait_ge(ready, at + k + 1)
                    for m in range(2):
                        for n, (w, x) in enumerate(((w_hi, x_hi), (w_lo, x_hi), (w_hi, x_lo))):
                            mm = pe.matmul(bank[2 * u + m], w[:, u, k, m * P:(m + 1) * P], x[:, k, :],
                                           start=(k == 0 and n == 0), stop=(k == KT - 1 and n == 2))
                        if k == KT - 1:
                            mm.then_inc(bank_full[2 * u + m], 1)

            def product(c, half, u, by_tokens=False, first=False, between=None,
                        source=(act_hi, act_lo), late=0):
                x_hi, x_lo = source
                pe.wait_ge(lo_done, c + 1)
                for m in range(2):
                    if not first:
                        pe.wait_ge(bank_free[2 * u + m], half)
                    b = bank[2 * u + m]
                    if by_tokens:
                        for t in range(2):
                            tok = slice((2 * m + t) * P, (2 * m + t + 1) * P)
                            for k in range(KT):
                                if late and m == 1 and KT * t + k == 2 * late:
                                    between()
                                for n, (x, w) in enumerate(((x_hi, w_hi), (x_hi, w_lo), (x_lo, w_hi))):
                                    mm = pe.matmul(b[:, t * CW:(t + 1) * CW], x[:, k, tok], w[:, u, k, :],
                                                   start=(k == 0 and n == 0), stop=(k == KT - 1 and n == 2))
                    else:
                        for k in range(KT):
                            if late and m == 1 and k == late:
                                between()
                            for n, (w, x) in enumerate(((w_hi, x_hi), (w_lo, x_hi), (w_hi, x_lo))):
                                mm = pe.matmul(b[:], w[:, u, k, m * P:(m + 1) * P], x[:, k, :],
                                               start=(k == 0 and n == 0), stop=(k == KT - 1 and n == 2))
                    mm.then_inc(bank_full[2 * u + m], 1)
                    if m == 0 and between is not None and not late:
                        between()

            def stream(c0, n, **kw):
                if n < 4:
                    for c in range(c0, c0 + n):
                        product(c, c // 2, c % 2, first=(c < 2), **kw)
                else:
                    with pe.Fori(0, n // 2) as i:
                        for v in range(2):
                            c = c0 + v
                            product(2 * i + c, i + c // 2, c % 2, **kw)

            def mean_square(n, squares):
                for k in range(KT):
                    x = squares(k)
                    pe.matmul(bank[4][:], ones[:], x, start=(k == 0), stop=(k == KT - 1)).then_inc(sq_used, 1)

            def out_product(c0, n, ready, at, squares):
                arriving(c0, ready, at)
                for j in range(1, 4):
                    product(c0 + j, (c0 + j) // 2, (c0 + j) % 2)
                for k in (0, 6, 7):
                    c = c0 + k // 2
                    if k:
                        pe.wait_ge(bank_free[2 * (c % 2) + k % 2], c // 2 + 1)
                    else:
                        pe.wait_ge(squares_summed, n)
                    pe.matmul(bank[4][:], ones[:], squares[:, k], start=(k == 0), stop=(k == KT - 1))\
                        .then_inc(sq_used, 1 if k else 6)

            def ring_squares(n):
                def at(k):
                    pe.wait_ge(sq_ready, KT * (n // 2) + k + 1)
                    return tmp[:, k % 2]
                return at

            pe.wait_ge(consts_ready, 1)
            for k in range(KT):
                pe.wait_ge(x_landed[k // 4], 16)
                if k >= 4:
                    pe.wait_ge(xt_copied, k - 3)
                for t in range(TT):
                    mm = pe.transpose(bank[4 + k % 4][:, t * P:(t + 1) * P], x_tok[:, t, k * P:(k + 1) * P], ident[:])
                mm.then_inc(xt_full, 1)
            pe.wait_ge(vec_landed, 16 * len(VECS))
            pe.transpose(bank[0][:, 0:NVEC], vec_rows[0:NVEC, :], ident[0:NVEC, 0:NVEC]).then_inc(vec_full, 1)
            pe.wait_ge(xt_copied, KT)
            mean_square(0, ring_squares(0))
            pe.wait_ge(vec_ready, 1)

            pe.wait_ge(lo_done, 1)
            for k in range(KT):
                pe.wait_ge(h_ready, k + 1)
                for n, (w, x) in enumerate(((w_hi, act_hi), (w_lo, act_hi), (w_hi, act_lo))):
                    mm = pe.matmul(bank[1][:], w[:, 0, k, 0:P], x[:, k, :],
                                   start=(k == 0 and n == 0), stop=(k == KT - 1 and n == 2))
            mm.then_inc(bank_full[1], 1)
            pe.sem_inc(bank_full[0], 1)
            stream(C_Q, 1)
            pe.wait_ge(bank_free[1], 1)
            pe.wait_ge(up_landed, 16)
            pe.wait_ge(rstd_ready, 1)
            for h in range(GH):
                pe.matmul(bank[4 + h][:], w_up[:, h * P:(h + 1) * P], glr_t[:], start=True, stop=True).then_inc(up_full, 1)
            stream(C_Q + 1, 1)
            stream(C_K, 2)
            stream(C_V, 4, by_tokens=True)

            def k_d_by_tokens():
                for h in range(GH):
                    pe.wait_ge(nu_ready, h + 1)
                    pe.wait_ge(kd_ready, h + 1)
                    for t in range(TT):
                        mm = pe.transpose(bank[4 + h][:, t * P:(t + 1) * P], kd_t[:, h, t * P:(t + 1) * P], ident[:])
                    mm.then_inc(kdt_full, 1)

            def chunk_scores():
                for h in range(GH):
                    pe.wait_ge(exps_used, h + 1)
                    pe.wait_ge(kdtok_ready, h + 1)
                    for t in range(TT):
                        tok = slice(t * P, (t + 1) * P)
                        mm = pe.matmul(bank[4 + h][:, tok], qk[:, GH + h, tok], qk[:, h, tok], start=True, stop=True)
                    mm.then_inc(att_full, 1)

            def updates(h):
                pe.wait_ge(kdtok_ready, GH if h == 0 else h + 1)
                if h:
                    pe.wait_ge(upd_read, h)
                for n in range(GN - 1):
                    r = slice(n % 2 * GC, n % 2 * GC + GC)
                    mm = pe.matmul(update_at(n), kd_tok[r, h, n // 2, :],
                                   v_tok[r, n // 2, h * GDV:(h + 1) * GDV], start=True, stop=True)
                mm.then_inc(upd_full, 1)

            def out_squares(t):
                h = t // 2
                pe.wait_ge(o_squared, t + 1)
                pe.matmul(bank[3][0:GH, :], head_sel[:, GH - 1 - h:2 * GH - 1 - h], tmp[:, t % 2],
                          start=(t == 0), stop=(t == 2 * GH - 1)).then_inc(osq_used, 1)

            product(C_Z, C_Z // 2, C_Z % 2)
            product(C_Z + 1, (C_Z + 1) // 2, (C_Z + 1) % 2, between=k_d_by_tokens)
            product(C_Z + 2, (C_Z + 2) // 2, (C_Z + 2) % 2, between=chunk_scores)

            def first_updates():
                pe.wait_ge(att_ready, GH)
                updates(0)
            product(C_Z + 3, (C_Z + 3) // 2, (C_Z + 3) % 2, between=first_updates)
            banks_free(pe, C_GOUT)
            for h in range(GH):
                if h < GH - 1:
                    updates(h + 1)
                for e in range(2):
                    t = 2 * h + e
                    if t >= 3:
                        pe.wait_ge(o_read, t - 2)
                    b = bank[t % 3]
                    ch = slice(h * GDV + e * P, h * GDV + (e + 1) * P)
                    for tt in range(TT):
                        tok = slice(tt * P, (tt + 1) * P)
                        mm = pe.matmul(b[:, tok], v_tok[:, tt, ch], att[:, h, tok], start=True, stop=False)
                        for n in range(2 * tt, 2 * tt + 2):
                            if n:
                                if e == 0:
                                    pe.wait_ge(state_ready, (GN - 1) * h + n)
                                q = slice(n * GC, (n + 1) * GC)
                                mm = pe.matmul(b[:, q], states[:, h % 2, n, e * P:(e + 1) * P], qk[:, h, q],
                                               start=False, stop=(n % 2 == 1))
                    mm.then_inc(o_full, 1)
                    if t:
                        out_squares(t - 1)
            out_squares(2 * GH - 1)
            pe.wait_ge(orstd_ready, 1)
            pe.wait_ge(upd_read, GH)
            for h in range(GH):
                pe.matmul(bank[4 + h][:], ident[0:GH, h:h + 1].broadcast_to([GH, P]), head_std[0:GH, :],
                          start=True, stop=True).then_inc(obc_full, 1)
            out_product(C_GOUT, 1, h_ready, KT, y_sq)

            pe.wait_ge(rstd_ready, 2)
            mean_square(2, ring_squares(2))
            pe.wait_ge(small2_landed, 16 * N_SMALL2)
            pe.transpose(bank[5][:, 0:CB], pe_rows, ident[0:CB, 0:CB]).then_inc(pe_full, 1)

            def turn(r0):
                for r in (r0, r0 + 1):
                    pe.wait_ge(turn_ready, r + 1)
                    if r >= 2:
                        pe.wait_ge(turned, r - 1)
                    else:
                        pe.wait_ge(pe_ready, 1)
                        pe.wait_ge(consts2_ready, 1)
                    pe.matmul(bank[4 + r % 2][:], perm[:], rope_at(r)[1][:, r % 2], start=True, stop=True).then_inc(turn_full, 1)

            def compress(c, part, i, between=None):
                pe.wait_ge(lo_done, c + 1)
                if part == 0:
                    pe.wait_ge(kv_split, i + 1)
                    if i:
                        pe.wait_ge(cmp_ready, 1)
                    else:
                        pe.wait_ge(consts2_ready, 1)
                u = c % 2
                for m in range(2):
                    for k in range(KT):
                        at = 2 * (KT * part + k)
                        for n, (w, x) in enumerate(((w_hi, kv_hi), (w_lo, kv_hi), (w_hi, kv_lo))):
                            mm = pe.matmul(bank[6 + m][:, 0:(NG + 1) * NCP].rearrange("p (g c) -> p g c", c=NCP),
                                           w[:, u, k, m * P:(m + 1) * P],
                                           x[:, :, at:at + CS * (NCP - 1) + 1:CS],
                                           start=(part == 0 and k == 0 and n == 0),
                                           stop=(part == 1 and k == KT - 1 and n == 2))
                    if m == 0 and between is not None:
                        between()
                mm.then_inc(bank_full[2 * u + 1], 1)
                pe.sem_inc(bank_full[2 * u], 1)

            arriving(C_KC, h_ready, 2 * KT)
            product(C_KS, C_KS // 2, C_KS % 2)
            product(C_VC, C_VC // 2, C_VC % 2, between=lambda: turn(0))
            product(C_KW, C_KW // 2, C_KW % 2, between=lambda: turn(2))
            compress(C_CK, 0, 0, between=lambda: turn(4))
            compress(C_CK + 1, 1, 0)
            product(C_VS, C_VS // 2, C_VS % 2, by_tokens=True)
            pe.wait_ge(hid_ready, 2)
            for m in range(2):
                for half in range(2):
                    mm = pe.matmul(bank[6][half * NDH:(half + 1) * NDH, 0:NG * NCP], w2k[:, m, :], hid[:, m, :],
                                   start=(m == 0), stop=(m == 1))
            mm.then_inc(cmp_full, 1)
            product(C_VW, C_VW // 2, C_VW % 2, by_tokens=True)
            compress(C_CV, 0, 1)
            compress(C_CV + 1, 1, 1)
            u = C_GL % 2
            pe.wait_ge(lo_done, C_GL + 1)
            pe.wait_ge(bank_free[2 * u + 1], C_GL // 2)
            for k in range(KT):
                for n, (w, x) in enumerate(((w_hi, act_hi), (w_lo, act_hi), (w_hi, act_lo))):
                    mm = pe.matmul(bank[2 * u + 1][0:48, :], w[:, u, k, 0:48], x[:, k, :],
                                   start=(k == 0 and n == 0), stop=(k == KT - 1 and n == 2))
            mm.then_inc(bank_full[2 * u + 1], 1)
            pe.sem_inc(bank_full[2 * u], 1)
            product(C_NQ, C_NQ // 2, C_NQ % 2)
            pe.wait_ge(hid_ready, 4)
            for g in range(NG):
                for m in range(2):
                    mm = pe.matmul(bank[6][:, g * NDH:(g + 1) * NDH],
                                   hid4[:, m, g * P:(g + 1) * P],
                                   w2v[:, m, :], start=(m == 0), stop=(m == 1))
            mm.then_inc(cmp_full, 1)
            pe.wait_ge(gates_t_ready, 1)
            for t in range(TT):
                mm = pe.transpose(bank[7][:, t * 48:(t + 1) * 48], gates_t[:, t * P:(t + 1) * P], ident[0:48, 0:48])
            mm.then_inc(gates_full, 1)
            for j in range(1, 4):
                product(C_NQ + j, (C_NQ + j) // 2, (C_NQ + j) % 2, between=lambda: turn(4 + 2 * j))
            pe.wait_ge(turn_ready, 14)
            turn(12)

            def scores(p):
                t, i = p // 8, p % 8
                tok = slice(t * P, (t + 1) * P)
                g = i // 4
                if p:
                    pe.wait_ge(s_exp, 4 * p)
                for kT in (ksT, kwT):
                    for half in range(2):
                        rows = slice(half * NDH, (half + 1) * NDH)
                        b = bank[2 * half + (kT is kwT)]
                        pe.matmul(b[:, 0:(t + 1) * P], qT[rows, i, tok], kT[rows, g, 0:(t + 1) * P], start=True, stop=False)
                for half in range(2):
                    for w in range(2):
                        mm = pe.matmul(bank[2 * half + w][:, t * P:(t + 1) * P], identb[:], maskb[:], start=False, stop=True)
                    mm.then_inc(s_full, 1)

            def turn_weights(n):
                t = n // 16
                pe.wait_ge(p_ready, n + 1)
                if n:
                    pe.wait_ge(t_sel, n)
                    pe.wait_ge(t_win, n)
                for w in range(2):
                    for k in range(t + 1):
                        mm = pe.transpose(bank[4 + w][:, k * P:(k + 1) * P], prob[:, n % 3, w, k * P:(k + 1) * P], ident[:])
                mm.then_inc(t_full, 1)

            def values(p):
                t, i = p // 8, p % 8
                a = i // 4
                pe.wait_ge(t_sel, 2 * p + 2)
                pe.wait_ge(t_win, 2 * p + 2)
                if p >= 2:
                    pe.wait_ge(pv_read, p - 1)
                for w in range(2):
                    for k in range(t + 1):
                        mm = pe.matmul(bank[6 + p % 2][:, 0:2 * P].rearrange("p (h q) -> p h q", h=2),
                                       v_tok2[:, k, w, 2 * a * NDH:(2 * a + 2) * NDH],
                                       probT[:, p % 2, :, w, k * P:(k + 1) * P],
                                       start=(w == 0 and k == 0), stop=(w == 1 and k == t))
                mm.then_inc(pv_full, 1)

            def modulation():
                pe.wait_ge(ada_summed, 1)
                for i in range(3 * KT):
                    mm = pe.matmul(bank[7][:, i:i + 1], ada_sum[:, i // 2, i % 2 * P:(i % 2 + 1) * P], ones[:, 0:1],
                                   start=True, stop=True)
                mm.then_inc(mod_full, 1)
                pe.wait_ge(mod_full, 1)
                for b in range(4):
                    pe.sem_inc(bank_full[b], (C_NOUT - C_ADA) // 2)

            def c_score(t):
                tok = slice(t * P, (t + 1) * P)
                if t == 0:
                    pe.wait_ge(turned, 14)
                    pe.wait_ge(cmp_ready, 2)
                for i in range(8):
                    for half in range(2):
                        rows = slice(half * NDH, (half + 1) * NDH)
                        g = 2 * (i // 4) + half
                        mm = pe.matmul(bank[4 + half][:, i * NCP:(i + 1) * NCP], qT[rows, i, tok],
                                       kcmpT[rows, g * NCP:(g + 1) * NCP], start=True, stop=True)
                mm.then_inc(c_scores, 1)

            def c_turn(t):
                pe.wait_ge(c_prob, t + 1)
                if t:
                    pe.wait_ge(c_taken, t)
                for g in range(NG):
                    pc = csc[:, 1].rearrange("p (h i c) -> p h i c", h=2, i=8)[:, g % 2, g // 2 * 4:g // 2 * 4 + 4, :]
                    mm = pe.transpose(bank[6][:, g * P:(g + 1) * P], pc.rearrange("p i c -> p (i c)"), ident[:])
                mm.then_inc(c_tfull, 1)

            def c_values(t):
                pe.wait_ge(c_tcopied, t + 1)
                for i in range(KT):
                    for half in range(2):
                        g, j = 2 * (i // 4) + half, i % 4
                        mm = pe.matmul(bank[6 + i // 4][half * NDH:(half + 1) * NDH, j * P:(j + 1) * P],
                                       vcmp[:, g, j * NDH:(j + 1) * NDH], pcT[:, g, :], start=True, stop=True)
                mm.then_inc(c_out, 1)

            for t in range(TT):
                c_score(t)
                c = C_NZ + t
                product(c, c // 2, c % 2, between=lambda: c_turn(t))
                c_values(t)
            banks_free(pe, C_ADA)
            pe.wait_ge(c_taken, TT)
            scores(0)
            for p in range(NPAIR):
                if p < NPAIR - 1:
                    scores(p + 1)
                turn_weights(2 * p)
                if p == MOD_PAIR:
                    pe.wait_ge(pv_read, p - 2)
                    modulation()
                    pe.wait_ge(mod_ready, 1)
                if p:
                    values(p - 1)
                turn_weights(2 * p + 1)
            values(NPAIR - 1)
            out_product(C_NOUT, 2, ot_low, 0, y_sq2)


            pe.wait_ge(rstd_ready, 4)
            mean_square(4, ring_squares(4))
            arriving(C_H, h_ready, 3 * KT)
            for c in range(C_H + 1, C_H + 4):
                product(c, c // 2, c % 2, by_tokens=(c == C_H + 2))

            def rows3(h):
                return slice(h % 2 * NDH, (h % 2 + 1) * NDH)

            def head_scores(h):
                s, tile = h // 4 % 2, h % 4 // 2
                for st in range(TT - 1, -1, -1):
                    if h:
                        pe.wait_ge(w_ready, TT * (h - 1) + TT - st)
                        if st == 0:
                            pe.wait_ge(head_gated, h)
                    b = bank[4 + st]
                    pe.matmul(b[:, st * P:S], kh[rows3(h), s, tile, st * P:(st + 1) * P], qh[rows3(h), s, tile, st * P:S],
                              start=True, stop=False)
                    pe.matmul(b[:, st * P:(st + 1) * P], identb3[:], maskb3[:], start=False, stop=True)\
                        .then_inc(z_full, 1)

            def head_sums(h):
                for i, st in enumerate(range(TT - 1, -1, -1)):
                    pe.wait_ge(sp_ready, TT * h + i + 1)
                    for jt in range(TT - 1, st - 1, -1):
                        for n, part in enumerate((sp_hi, sp_lo)):
                            mm = pe.matmul(bank[4 + st][:, jt * P:S], (tri_r if jt == st else minus_r)[:], blocks(part, jt),
                                           start=False, stop=(jt == st and n == 1), skip_group_check=True)
                    mm.then_inc(tri_full, 1)

            def head_values(h):
                s = h // 4 % 2
                pe.wait_ge(w_ready, TT * (h + 1))
                for st in range(TT):
                    mm = pe.matmul(bank[4][rows3(h), st * P:S], vh[:, s, st, h % 4 * NDH:(h % 4 + 1) * NDH], blocks(w_z, st),
                                   start=(st == 0), stop=(st == TT - 1))
                mm.then_inc(hv_full, 1)

            pe.wait_ge(consts3_ready, 1)
            banks_free(pe, C_H + 4)
            for h in range(HH):
                c = C_H + 4 + h
                head_scores(h)
                product(c, c // 2, c % 2, by_tokens=(c < C_MA and h % 4 == 2), between=lambda: head_sums(h), late=4)
                head_values(h)
            stream(C_U, 4)
            pe.wait_ge(pair_low, KT)
            stream(C_BA, 4, source=(br_hi, br_lo))
            stream(C_ZB, 4)
            stream(C_MB, 4)
            c, u = C_MIX, C_MIX % 2
            pe.wait_ge(lo_done, c + 1)
            pe.wait_ge(d_low, KT)
            pe.wait_ge(head_gated, HH)
            for tile in range(KT):
                if tile >= 4:
                    pe.wait_ge(mix_taken, tile - 3)
                for i in range(2):
                    k = tile // 2 * 2 + i
                    for n, (w, x) in enumerate(((w_hi, br_hi), (w_lo, br_hi), (w_hi, br_lo))):
                        mm = pe.matmul(bank[4 + tile % 4], w[:, u, k, tile % 2 * P:(tile % 2 + 1) * P], x[:, k, :],
                                       start=(i == 0 and n == 0), stop=(i == 1 and n == 2))
                mm.then_inc(mix_full if tile < KT - 1 else bank_full[2 * u + 1], 1)
            pe.sem_inc(bank_full[2 * u], 1)
            arriving(C_BB, h_ready, 4 * KT)
            for c in range(C_BB + 1, C_BB + 4):
                product(c, c // 2, c % 2)
            arriving(C_OUT, h_ready, 5 * KT, source=(br_hi, br_lo))
            pe.wait_ge(mix_taken, KT)

            for c in range(C_OUT + 1, C_END):
                product(c, c // 2, c % 2, source=(br_hi, br_lo))
            pe.wait_ge(squares_summed, 3)
            for k in (0, 6, 7):
                pe.wait_ge(sq_ready, KT * 3 + k + 1)
                pe.matmul(bank[4][:], ones[:], x_sq[:, k], start=(k == 0), stop=(k == KT - 1)).then_inc(sq_used, 1 if k else 6)
            for g in range(2):
                pe.wait_ge(fin_ready, 4 * (g + 1))
                for t in range(TT):
                    for k in range(4):
                        mm = pe.transpose(bank[4 * g + t][:, k * P:(k + 1) * P],
                                          xT[:, 4 * g + k, t * P:(t + 1) * P], ident[:])
                    mm.then_inc(out_full, 1)

        @block.vector
        def _(dve):
            chained = [0]

            def link(ins):
                chained[0] += 1
                ins.then_inc(dve_chain, 1)
                dve.wait_ge(dve_chain, chained[0])

            def inverse_root(n):
                dve.wait_ge(rstd_ready, n + 1)

            def split_act(n, scale, to=(act_hi, act_lo), shift=None):
                hi, lo = to

                def low(k):
                    dve.wait_ge(act_hi_done, KT * n + k + 1)
                    if shift is None:
                        low_part = dve.tensor_tensor(lo[:, k], tmp[:, k % 2], hi[:, k].bitcast(F32), ALU.subtract)
                    else:
                        low_part = dve.scalar_tensor_tensor(lo[:, k], tmp[:, k % 2], shift[:, k:k + 1],
                                                            hi[:, k].bitcast(F32), ALU.add, ALU.subtract)
                    low_part.then_inc(h_ready, 1)
                for k in range(KT):
                    if k >= 2:
                        dve.wait_ge(h_ready, KT * n + k - 1)
                    scale(k).then_inc(scaled, 1)
                    if k:
                        low(k - 1)
                low(KT - 1)

            for k in range(KT):
                dve.wait_ge(xt_full, k + 1)
                dve.tensor_copy(xT[:, k], bank[4 + k % 4][:]).then_inc(xt_copied, 1)
            dve.wait_ge(vec_full, 1)
            dve.tensor_copy(vec[:], bank[0][:, 0:NVEC]).then_inc(vec_ready, 1)
            dve.wait_ge(vec_ready, 1)
            dve.tensor_scalar(neg_bgk[:], vec[:, VAT["b_gk"]:VAT["b_gk"] + GH], -1.0, None, ALU.mult)
            inverse_root(0)
            split_act(0, lambda k: dve.scalar_tensor_tensor(tmp[:, k % 2], xT[:, k], vcol("pre0", k), rstd[:],
                                                            ALU.mult, ALU.mult))
            for h in range(GH):
                dve.wait_ge(up_full, h + 1)
                link(dve.tensor_scalar(gate_b[:, h], bank[4 + h][:], -1.0, neg_bgk[:, h:h + 1], ALU.mult, ALU.add))
                dve.tensor_scalar(kd_t[:, h], gate_b[:, h], CAP, None, ALU.min).then_inc(nu_ready, 1)
            for h in range(GH):
                g = gate_b[:, h].rearrange("p (n c) -> p n c", c=GC)
                dve.wait_ge(ln_ready, h + 1)
                link(dve.tensor_tensor(gate_b[:, h], kd_t[:, h], gate_b[:, h], ALU.max))
                dve.tensor_tensor_scan(gate_b[:, h], chunk_keep[:], gate_b[:, h], 0.0, ALU.mult,
                                       ALU.add).then_inc(gsum_ready, 1)
                dve.wait_ge(gsum_ready, h + 1)
                dve.tensor_tensor(kd_t[:, h].rearrange("p (n c) -> p n c", c=GC), g,
                                  g[:, :, GC - 1:GC].broadcast_to([P, GN, GC]), ALU.subtract).then_inc(grow_ready, 1)
            for h in range(GH):
                dve.wait_ge(exps_ready, h + 1)
                if h == 0:
                    banks_free(dve, C_K + 2)
                e = exps[:, h % 2]
                dve.tensor_tensor(qk[:, h], qk[:, h], e[:, 0], ALU.mult)
                dve.tensor_copy(decay[:, h].rearrange("p (n o) -> p n o", o=1),
                                e[:, 0].rearrange("p (n c) -> p n c", c=GC)[:, :, GC - 1:GC])
                link(dve.tensor_tensor(kd_t[:, h], qk[:, GH + h], e[:, 2], ALU.mult))
                dve.sem_inc(kd_ready, 1)
                dve.tensor_tensor(qk[:, GH + h], qk[:, GH + h], e[:, 1], ALU.mult).then_inc(exps_used, 1)
            for h in range(GH):
                dve.wait_ge(att_full, h + 1)
                dve.copy_predicated(att[:, h].rearrange("p (t i) -> p t i", i=P),
                                    causal[:].rearrange("p (o i) -> p o i", o=1).broadcast_to([P, TT, P]),
                                    bank[4 + h][:].rearrange("p (t i) -> p t i", i=P)).then_inc(att_ready, 1)
            def take_out(t):
                dve.wait_ge(o_squared, t + 1)
                dve.scalar_tensor_tensor(o_t[:, t], bank[t % 3][:], vcol("head_norm", t % 2), silu_z[:, t],
                                         ALU.mult, ALU.mult).then_inc(o_read, 1)
            for h in range(GH):
                dve.wait_ge(upd_full, h + 1)
                if h >= 2:
                    dve.wait_ge(o_full, 2 * (h - 1))
                for n in range(1, GN):
                    upd = update_at(n - 1)
                    if n == 1:
                        dve.tensor_copy(states[:, h % 2, n], upd).then_inc(state_ready, 1)
                    else:
                        dve.wait_ge(state_ready, (GN - 1) * h + n - 1)
                        dve.scalar_tensor_tensor(states[:, h % 2, n], states[:, h % 2, n - 1], decay[:, h, n - 1:n], upd,
                                                 ALU.mult, ALU.add).then_inc(state_ready, 1)
                dve.wait_ge(state_ready, (GN - 1) * (h + 1))
                dve.sem_inc(upd_read, 1)
                if h:
                    take_out(2 * h - 2)
                    take_out(2 * h - 1)
            take_out(2 * GH - 2)
            take_out(2 * GH - 1)
            dve.wait_ge(obc_full, GH)
            dve.wait_ge(osq_used, 2 * GH)
            dve.wait_ge(o_read, 2 * GH)
            split_act(1, lambda k: dve.tensor_tensor(tmp[:, k % 2], o_t[:, k], bank[4 + k // 2][:], ALU.mult))

            def sum_squares(c0, squares):
                for k in range(6):
                    c = c0 + k // 2
                    dve.wait_ge(bank_free[2 * (c % 2) + k % 2], c // 2 + 1)
                    if k:
                        link(dve.tensor_tensor(squares[:, 0], squares[:, 0], squares[:, k], ALU.add))
                dve.sem_inc(squares_summed, 1)

            def residual(n, name, y):
                inverse_root(n)
                for k in range(KT):
                    dve.scalar_tensor_tensor(y[:, k], y[:, k], vcol(name, k), rstd[:], ALU.mult, ALU.mult).then_inc(y_scaled, 1)
                    if k % 2:
                        dve.wait_ge(y_scaled, KT * (n // 2) + k)
                        dve.tensor_tensor(xT[:, k - 1], xT[:, k - 1], y[:, k - 1], ALU.add).then_inc(x_even, 1)
            sum_squares(C_GOUT, y_sq)
            residual(1, "post0", y_t)

            inverse_root(2)
            dve.wait_ge(pe_full, 1)
            dve.tensor_copy(pe_t[:].rearrange("p i m -> p (i m)"), bank[5][:, 0:CB]).then_inc(pe_ready, 1)
            split_act(2, lambda k: dve.scalar_tensor_tensor(tmp[:, k % 2], xT[:, k], vcol("pre1", k), rstd[:],
                                                            ALU.mult, ALU.mult))

            dve.wait_ge(small2_landed, 16 * N_SMALL2)
            pos, turns = rope_a[:, 0], rope_b[:, 0]
            link(dve.tensor_copy(rope_a[:, 1], pos.bitcast(I32)))
            link(dve.tensor_scalar(rope_a[:, 1], rope_a[:, 1], rope_c[:, 0:1], None, ALU.mult))
            for tab, shift in ((sinT, 0.0), (cosT, 0.25)):
                link(dve.tensor_scalar(turns, rope_a[:, 1], 1.0 / (2.0 * np.pi), shift, ALU.mult, ALU.add))
                link(dve.tensor_scalar(turns, turns, ROUND, -ROUND, ALU.add, ALU.add))
                src = rope_a[:, 1]
                for part in TWO_PI:
                    link(dve.scalar_tensor_tensor(tab[:], turns, -part, src, ALU.mult, ALU.add))
                    src = tab[:]
                link(dve.tensor_scalar(tab[:], tab[:], 2.0 * np.pi * shift, PI_DOWN, ALU.add, ALU.min))
                dve.tensor_scalar(tab[:], tab[:], -PI_DOWN, None, ALU.max).then_inc(angle_ready, 1)
            def turn_parts(c, r0):
                for m in range(2):
                    b = 2 * (c % 2) + m
                    dve.wait_ge(bank_full[b], c // 2 + 1)
                    cos_part, sin_part = rope_at(r0)
                    dve.tensor_tensor(cos_part[:, m], bank[b][:], cosT[:], ALU.mult)
                    link(dve.tensor_tensor(sin_part[:, m], bank[b][:], sinT[:], ALU.mult))
                    dve.sem_inc(turn_ready, 1)
                    dve.sem_inc(bank_free[b], 1)

            def turn_sum(r0, dst):
                for m in range(2):
                    dve.wait_ge(turn_full, r0 + m + 1)
                    dve.tensor_tensor(dst(m), rope_at(r0)[0][:, m], bank[4 + m][:], ALU.add).then_inc(turned, 1)

            def kv_low(i):
                dve.wait_ge(kv_hi_done, i + 1)
                dve.tensor_tensor(kv_lo[:, 0:NG], kv_full[:], kv_hi[:, 0:NG].bitcast(F32), ALU.subtract)
                dve.tensor_tensor(kv_lo[:, NG, 0:CB:2], pe_t[:, i], kv_hi[:, NG, 0:CB:2].bitcast(F32),
                                  ALU.subtract).then_inc(kv_split, 1)

            def hidden_bias(i):
                for m in range(2):
                    c = (C_CK, C_CV)[i] + 1
                    dve.wait_ge(bank_full[2 * (c % 2) + 1], c // 2 + 1)
                    link(dve.tensor_copy(hid_bias[:, m:m + 1], bank[6 + m][:, NG * NCP:NG * NCP + 1]))
                dve.sem_inc(hid_bias_ready, 1)

            dve.wait_ge(table_ready, 2)
            turn_parts(C_KC, 0)
            turn_parts(C_KS, 2)
            for m in range(2):
                dve.wait_ge(turn_full, m + 1)
                for g in range(2):
                    a = rope_a[g * NDH:(g + 1) * NDH, m]
                    b = bank[4 + m][g * NDH:(g + 1) * NDH, :]
                    dve.tensor_tensor(kv_full[0:NDH, 2 * m + g, 0:S], a, b, ALU.add)
                    last = dve.tensor_tensor(kv_full[NDH:P, 2 * m + g, 0:S - 1], a[:, 1:S], b[:, 1:S], ALU.add)
                last.then_inc(turned, 1)
            dve.wait_ge(turned, 2)
            dve.sem_inc(kv_ready, 1)
            kv_low(0)
            turn_sum(2, lambda m: ksT[:, m])
            turn_parts(C_KW, 4)
            turn_sum(4, lambda m: kwT[:, m])
            hidden_bias(0)
            kv_low(1)
            dve.wait_ge(cmp_full, 1)
            dve.tensor_copy(kcmpT[:], bank[6][:, 0:NG * NCP]).then_inc(cmp_ready, 1)
            hidden_bias(1)
            turn_parts(C_NQ, 6)
            dve.wait_ge(cmp_full, 2)
            for h in range(NHG):
                r = slice(h * NCP, (h + 1) * NCP)
                last = dve.tensor_copy(vcmp[r, :, h * NDH:(h + 1) * NDH],
                                       bank[6][r, 0:CW].rearrange("p (g d) -> p g d", g=NG))
            last.then_inc(cmp_ready, 1)
            dve.wait_ge(gates_full, 1)
            dve.tensor_copy(gates[:].rearrange("p t n -> p (t n)"), bank[7][:, 0:TT * 48]).then_inc(gate_ready, 1)
            for j in range(4):
                turn_sum(6 + 2 * j, lambda m: qT[:, 2 * j + m])
                if j < 3:
                    turn_parts(C_NQ + j + 1, 8 + 2 * j)
            dve.wait_ge(gate_ready, 1)

            def compressed(t):
                heads = lambda a: a.rearrange("p (h c) -> p h c", c=NCP)
                over_heads = lambda a, n: a.rearrange("p (o c) -> p o c", o=1).broadcast_to([P, n, NCP])
                over_blocks = lambda a: a.rearrange("p (h o) -> p h o", o=1).broadcast_to([P, 16, NCP])
                dve.wait_ge(c_scores, t + 1)
                if t:
                    dve.wait_ge(c_tfull, t)
                for half in range(2):
                    link(dve.tensor_tensor(heads(csc[:, 0, half * CW:(half + 1) * CW]), heads(bank[4 + half][:, 0:CW]),
                                           over_heads(cmask[:, t], 8), ALU.add))
                link(dve.tensor_reduce(cstat[:, 0], heads(csc[:, 0]), AX_X, ALU.max))
                dve.tensor_tensor(heads(csc[:, 0]), heads(csc[:, 0]), over_blocks(cstat[:, 0]), ALU.subtract).then_inc(c_shifted, 1)
                dve.wait_ge(c_exp, t + 1)
                link(dve.tensor_tensor(heads(csc[:, 1]), heads(csc[:, 1]), over_heads(cvalid[:, t], 16), ALU.mult))
                link(dve.tensor_reduce(cstat[:, 1], heads(csc[:, 1]), AX_X, ALU.add))
                link(dve.tensor_scalar(cstat[:, 1], cstat[:, 1], 1e-30, None, ALU.max))
                link(dve.reciprocal(cstat[:, 1], cstat[:, 1]))
                for half in range(2):
                    g = gates[:, t].rearrange("p (a h j c) -> p a h j c", a=2, h=2, j=4)[:, :, half, :, 0]
                    o = cstat[:, 2, 8 * half:8 * half + 8].rearrange("p (a j) -> p a j", a=2)
                    i = cstat[:, 1, 8 * half:8 * half + 8].rearrange("p (a j) -> p a j", a=2)
                    link(dve.tensor_tensor(o, i, g, ALU.mult))
                dve.tensor_tensor(heads(csc[:, 1]), heads(csc[:, 1]), over_blocks(cstat[:, 2]), ALU.mult).then_inc(c_prob, 1)
                dve.wait_ge(c_out, t + 1)
                for b in range(2):
                    last = dve.tensor_copy(oT[:, 4 * b:4 * b + 4, t * P:(t + 1) * P],
                                           bank[6 + b].rearrange("p (k q) -> p k q", q=P))
                link(last)
                dve.sem_inc(c_taken, 1)

            def unit_max(n):
                t = n // 16
                dve.wait_ge(s_full, n + 1)
                st = wstat[:, n % 4]
                link(dve.tensor_reduce(st[:, :, 0], banks[:, 2 * (n % 2):2 * (n % 2) + 2, 0:(t + 1) * P], AX_X, ALU.max))
                dve.tensor_scalar(st[:, :, 1], st[:, :, 0], -NDH ** -0.5, None, ALU.mult).then_inc(s_max, 1)

            def unit_weights(n):
                t, i, half = n // 16, n % 16 // 2, n % 2
                h = i // 4 * 8 + half * 4 + i % 4
                st = wstat[:, n % 4]
                dve.wait_ge(s_exp, 2 * n + 2)
                link(dve.reciprocal(st[:, :, 3], st[:, :, 2]))
                link(dve.tensor_tensor(st[:, :, 3], st[:, :, 3], gates[:, t, 3 * h + 1:3 * h + 3], ALU.mult))
                for w in range(2):
                    p = prob[:, n % 3, w, 0:(t + 1) * P]
                    last = dve.tensor_scalar(p, p, st[:, w, 3:4], None, ALU.mult)
                last.then_inc(p_ready, 1)

            def unit_turned(n):
                w = (n // 16 + 1) * P
                dve.wait_ge(t_full, n + 1)
                if n >= 4:
                    dve.wait_ge(pv_full, n // 2 - 1)
                dve.tensor_copy(probT[:, n // 2 % 2, n % 2, 1, 0:w], bank[5][:, 0:w]).then_inc(t_win, 1)

            def pair_out(p):
                t, i = p // 8, p % 8
                dve.wait_ge(pv_full, p + 1)
                for half in range(2):
                    o = oT[half * NDH:(half + 1) * NDH, i, t * P:(t + 1) * P]
                    last = dve.tensor_tensor(o, o, bank[6 + p % 2][half * NDH:(half + 1) * NDH, half * P:(half + 1) * P], ALU.add)
                last.then_inc(pv_read, 1)

            for t in range(TT):
                compressed(t)
            for n in range(2 * NPAIR + 4):
                if n % 2 == 0:
                    if 1 <= n < 2 * NPAIR + 1:
                        unit_weights(n - 1)
                    if 3 <= n < 2 * NPAIR + 3:
                        unit_turned(n - 3)
                    if n < 2 * NPAIR:
                        unit_max(n)
                    if n >= 2 and n < 2 * NPAIR + 2:
                        unit_turned(n - 2)
                    if n < 2 * NPAIR:
                        unit_max(n + 1)
                elif n < 2 * NPAIR + 1:
                    unit_weights(n - 1)
                if n == 2 * MOD_PAIR + 3:
                    dve.wait_ge(mod_full, 1)
                    dve.tensor_tensor(mod[:], bank[7][:, 0:3 * KT], vec[:, VAT["b_ada"]:VAT["b_ada"] + 3 * KT],
                                      ALU.add).then_inc(mod_ready, 1)
                if n >= 5 and n % 2:
                    pair_out((n - 5) // 2)
                if n >= 5 and n % 2 and (n - 5) // 2 % 8 == 7:
                    t = (n - 5) // 16
                    dve.wait_ge(pv_read, 8 * (t + 1))
                    if t == 0:
                        banks_free(dve, C_ADA)
                    o = oT[:, :, t * P:(t + 1) * P]
                    dve.tensor_tensor(o, o, silu_z2[:, :, t * P:(t + 1) * P], ALU.mult).then_inc(o_gated, 1)
            for k in range(KT):
                dve.wait_ge(ot_high, k + 1)
                dve.tensor_tensor(act_lo[:, k], oT[:, k], act_hi[:, k].bitcast(F32), ALU.subtract).then_inc(ot_low, 1)
            sum_squares(C_NOUT, y_sq2)
            residual(3, "post1", y_t2)

            dve.wait_ge(mod_ready, 1)
            link(dve.scalar_tensor_tensor(gain_mod[:], mod[:, KT:2 * KT], 1.0, vec[:, VAT["gain2"]:VAT["gain2"] + KT],
                                          ALU.add, ALU.mult))
            inverse_root(4)

            def modulated(k):
                return dve.scalar_tensor_tensor(tmp[:, k % 2], xT[:, k], gain_mod[:, k:k + 1], rstd[:], ALU.mult, ALU.mult)
            split_act(3, modulated, shift=mod)

            def pair_part(p):
                dve.wait_ge(pair_high, p + 1)
                dve.tensor_tensor(br_lo[:, p], gated[:, p % 2], br_hi[:, p].bitcast(F32), ALU.subtract).then_inc(pair_low, 1)

            for h in range(HH):
                r = slice(h % 2 * NDH, (h % 2 + 1) * NDH)
                for i, st in enumerate(range(TT - 1, -1, -1)):
                    dve.wait_ge(z_full, TT * h + i + 1)
                    dve.tensor_scalar(blocks(ln_z, st), bank[4 + st][:, st * P:S], CAP, None, ALU.min).then_inc(zc_ready, 1)
                for i, st in enumerate(range(TT - 1, -1, -1)):
                    dve.wait_ge(l_ready, TT * h + i + 1)
                    if h:
                        dve.wait_ge(tri_full, TT * h)
                    link(dve.tensor_tensor(blocks(ln_z, st), blocks(ln_z, st), bank[4 + st][:, st * P:S], ALU.max))
                    link(dve.tensor_copy(blocks(sp_hi, st), blocks(ln_z, st)))
                    dve.tensor_tensor(blocks(sp_lo, st), blocks(ln_z, st), blocks(sp_hi, st).bitcast(F32),
                                      ALU.subtract).then_inc(sp_ready, 1)
                if h % 2 == 0 and h:
                    pair_part(h // 2 - 1)
                dve.wait_ge(hv_full, h + 1)
                dve.tensor_tensor(gated[r, h // 2 % 2], bank[4][r, :], zh[r, h // 4 % 2, h % 4 // 2], ALU.mult)\
                    .then_inc(head_gated, 1)
            pair_part(HH // 2 - 1)

            dve.wait_ge(small3_landed, 16)
            for g, window in enumerate(WINDOWS):
                c = C_U + g
                u = pool_u[:, 2 * g:2 * g + 2]
                for m in range(2):
                    b = 2 * (c % 2) + m
                    dve.wait_ge(bank_full[b], c // 2 + 1)
                    link(dve.tensor_copy(u[:, m], bank[b]))
                    dve.sem_inc(bank_free[b], 1)
                src, step, n = u, 1, 0
                while step < window:
                    dst = sums[n % 2]
                    dve.tensor_copy(dst[:, :, 0:step], src[:, :, 0:step])
                    link(dve.tensor_tensor(dst[:, :, step:S], src[:, :, step:S], src[:, :, 0:S - step], ALU.add))
                    src, step, n = dst, 2 * step, n + 1
                link(dve.tensor_tensor(src[:, :, 0:16], src[:, :, 0:16],
                                       pool_fix[:, g:g + 1].broadcast_to([P, 2, 16]), ALU.mult))
                link(dve.scalar_tensor_tensor(u, src[:], 1.0 / window, u, ALU.mult, ALU.subtract))
                dve.sem_inc(d_ready, 1)
            with dve.Fori(0, 2) as i:
                for v in range(2):
                    c = C_BA + v
                    for m in range(2):
                        b = 2 * (c % 2) + m
                        dve.wait_ge(bank_full[b], i + (c // 2 + 1))
                        part = mix_a[:, bass.ds(4 * i + (2 * v + m), 1), :]
                        dve.tensor_tensor(part, part, bank[b].rearrange("p (o s) -> p o s", o=1), ALU.mult).then_inc(bank_free[b], 1)
            for k in range(KT):
                dve.wait_ge(d_high, k + 1)
                dve.tensor_tensor(br_lo[:, k], pool_u[:, k], br_hi[:, k].bitcast(F32), ALU.subtract).then_inc(d_low, 1)

            def pooled(k):
                if k < KT - 1:
                    dve.wait_ge(mix_full, k + 1)
                else:
                    dve.wait_ge(bank_full[2 * (C_MIX % 2) + 1], C_MIX // 2 + 1)
                link(dve.scalar_tensor_tensor(tmp[:, k % 2], bank[4 + k % 4], vcol("pool_scale", k), silu_zb[:, k],
                                              ALU.mult, ALU.mult))
                dve.sem_inc(mix_taken, 1)
                return dve.engine_nop()
            banks_free(dve, C_MIX)
            split_act(4, pooled)

            def merged(k):
                c = C_BB + k // 2
                b = 2 * (c % 2) + k % 2
                dve.wait_ge(bank_full[b], c // 2 + 1)
                link(dve.tensor_tensor(tmp[:, k % 2], bank[b], mix_b[:, k], ALU.mult))
                dve.sem_inc(bank_free[b], 1)
                return dve.tensor_tensor(tmp[:, k % 2], tmp[:, k % 2], mix_a[:, k], ALU.add)
            split_act(5, merged, (br_hi, br_lo))
            for k in range(KT):
                c = C_OUT + k // 2
                b = 2 * (c % 2) + k % 2
                dve.wait_ge(bank_full[b], c // 2 + 1)
                link(dve.scalar_tensor_tensor(xT[:, k], bank[b], mod[:, 2 * KT + k:2 * KT + k + 1], xT[:, k],
                                              ALU.mult, ALU.add))
                dve.sem_inc(x_final, 1)
                dve.sem_inc(bank_free[b], 1)
                if 2 <= k < 7:
                    dve.wait_ge(sq_ready, KT * 3 + k)
                    link(dve.tensor_tensor(x_sq[:, 0], x_sq[:, 0], x_sq[:, k - 1], ALU.add))
            dve.sem_inc(squares_summed, 1)
            inverse_root(5)
            for k in range(KT):
                dve.scalar_tensor_tensor(xT[:, k], xT[:, k], vcol("final", k), rstd[:], ALU.mult, ALU.mult).then_inc(fin_ready, 1)
            for t in (0, 2):
                dve.wait_ge(out_full, TT + t + 1)
                dve.tensor_copy(out_tok[:, t, S:D], bank[4 + t]).then_inc(out_right, 1)


_INS = ["x", "positions", "pre_norm", "post_norm", "gla_w_in", "gla_w_gk_up", "gla_b_gk", "gla_head_norm", "gla_w_out",
        "nsa_w_in", "nsa_b_gate", "nsa_pe_k", "nsa_pe_v", "nsa_ck_w1", "nsa_ck_w2", "nsa_cv_w1", "nsa_cv_w2",
        "nsa_w_out", "c_2", "norm_gain_2", "w_ada_2", "b_ada_2", "w_in_2", "pool_w_2", "pool_scale_2",
        "w_branch_a_2", "w_branch_b_2", "w_out_2", "final_gain_2"]


def named(aps):
    A = {}
    for name, a in aps.items():
        if a.shape[0] == 1:
            a = a[0]
        A[name] = a
    A["pre0"], A["pre1"], A["post0"], A["post1"] = (aps["pre_norm"][0], aps["pre_norm"][1], aps["post_norm"][0],
                                                    aps["post_norm"][1])
    A["gain2"], A["final"], A["b_ada"], A["pool_scale"] = (A["norm_gain_2"], A["final_gain_2"], A["b_ada_2"],
                                                           A["pool_scale_2"])
    A["pool_w_2"] = A["pool_w_2"].rearrange("g c d -> (g c) d")
    A["c"], A["b_gk"], A["head_norm"] = A["c_2"], A["gla_b_gk"], A["gla_head_norm"]
    return A


def shape_constants():
    half = NDH // 2
    inv = 10000.0 ** (-np.arange(0, NDH, 2, dtype=np.float64) / NDH)
    sign = np.where(np.arange(P) % NDH < half, 1.0, -1.0)
    t = np.arange(1, 17)
    return {"rope_const": np.stack([np.tile(inv, P // half), sign], axis=1).astype(np.float32),
            "pool_const": np.stack([w / np.minimum(t, w) for w in WINDOWS]).astype(np.float32)}


def kernel(**inputs):
    import numpy as _np
    import concourse.bacc as _bacc
    from concourse import mybir as _mybir
    from concourse.bass_utils import run_bass_kernel_spmd as _run

    nc = _bacc.Bacc("TRN2", target_bir_lowering=False, num_devices=1)
    arrays = {name: _np.ascontiguousarray(inputs[name]) for name in _INS}
    arrays.update(shape_constants())
    aps = {name: nc.dram_tensor(name, a.shape, _mybir.dt.from_np(a.dtype), kind="ExternalInput").ap()
           for name, a in arrays.items()}
    out = nc.dram_tensor("out", (1, S, D), _mybir.dt.float32, kind="ExternalOutput").ap()
    build_program(nc, named(aps), out[0])
    r = _run(nc, [arrays], core_ids=[0])
    return r.results[0]["out"]
```
